# Optimizing a Trainium2 kernel written in Bass

```python
import math
import jax, jax.numpy as jnp
from jax import lax
import numpy as np

D_MODEL = 1024
BATCH = 1
SEQ = 2048
DEPTH = 1
DEC_BATCH = 8
DEC_SEQ = 8
PAST_LEN = 4096
PAGE_SIZE = 128

HEAD_DIM = 64
ATTN_WIDTH = D_MODEL // 2
N_HEADS = ATTN_WIDTH // HEAD_DIM
N_KV_HEADS = 2
Q_PER_KV = N_HEADS // N_KV_HEADS
KV_WIDTH = N_KV_HEADS * HEAD_DIM
N_IDX_HEADS = 4
IDX_DIM = 64
TOPK_MAX = 256
Q_BLOCK = 128
ROPE_THETA = 10000.0
SSM_WIDTH = D_MODEL - ATTN_WIDTH
SSM_GROUP = 16
N_SSM_GROUPS = SSM_WIDTH // SSM_GROUP
SSM_STATE = 64
DT_MIN = 1e-3
DT_MAX = 1e-1
D_FF = 4 * D_MODEL
RMS_EPS = 1e-6
NEG = -1e30
OFF_Q = 0
OFF_K = OFF_Q + ATTN_WIDTH
OFF_V = OFF_K + KV_WIDTH
OFF_QI = OFF_V + KV_WIDTH
OFF_KI = OFF_QI + N_IDX_HEADS * IDX_DIM
OFF_WI = OFF_KI + IDX_DIM
OFF_U = OFF_WI + N_IDX_HEADS
IN_WIDTH = OFF_U + SSM_WIDTH

kernel_name = 'hymba_dsa_s5_decoder_step'

def rmsnorm(x, g):
    xf = x.astype(jnp.float32)
    y = xf * lax.rsqrt(jnp.mean(xf * xf, axis=-1, keepdims=True) + RMS_EPS)
    return (y * g.astype(jnp.float32)).astype(x.dtype)

def rope(x, pos):
    half = x.shape[-1] // 2
    inv = ROPE_THETA ** (-jnp.arange(half, dtype=jnp.float32) / half)
    ang = pos.astype(jnp.float32)[:, None] * inv[None, :]
    cos = jnp.cos(ang)[None, :, None, :]
    sin = jnp.sin(ang)[None, :, None, :]
    xf = x.astype(jnp.float32)
    x1, x2 = xf[..., :half], xf[..., half:]
    return jnp.concatenate([x1 * cos - x2 * sin, x1 * sin + x2 * cos], axis=-1).astype(x.dtype)

def mixer_inputs(x, pos, g_pre, w_in):
    B, T, _ = x.shape
    proj = rmsnorm(x, g_pre) @ w_in
    q = rope(proj[..., OFF_Q:OFF_K].reshape(B, T, N_HEADS, HEAD_DIM), pos)
    k = rope(proj[..., OFF_K:OFF_V].reshape(B, T, N_KV_HEADS, HEAD_DIM), pos)
    v = proj[..., OFF_V:OFF_QI].reshape(B, T, N_KV_HEADS, HEAD_DIM)
    qi = rope(proj[..., OFF_QI:OFF_KI].reshape(B, T, N_IDX_HEADS, IDX_DIM), pos)
    ki = rope(proj[..., OFF_KI:OFF_WI].reshape(B, T, 1, IDX_DIM), pos)[:, :, 0]
    wi = proj[..., OFF_WI:OFF_U]
    u = proj[..., OFF_U:]
    return q, k, v, qi, ki, wi, u

def indexer_topk(qi, wi, ki, q_pos, topk):
    s = jnp.einsum('bqhd,bld->bqhl', qi.astype(jnp.float32), ki.astype(jnp.float32)) * (IDX_DIM ** -0.5)
    score = jnp.einsum('bqhl,bqh->bql', jax.nn.relu(s), wi.astype(jnp.float32)) * (N_IDX_HEADS ** -0.5)
    key_pos = jnp.arange(ki.shape[1], dtype=jnp.int32)
    admissible = key_pos[None, :] <= q_pos[:, None]
    score = jnp.where(admissible[None], score, -jnp.inf)
    _, idx = lax.top_k(score, topk)
    valid = idx <= q_pos[None, :, None]
    return idx, valid

def sparse_attend(q, kg, vg, valid):
    B, Q = q.shape[:2]
    qg = q.reshape(B, Q, N_KV_HEADS, Q_PER_KV, HEAD_DIM).astype(jnp.float32)
    logits = jnp.einsum('bqngd,bqknd->bqngk', qg, kg.astype(jnp.float32)) * (HEAD_DIM ** -0.5)
    logits = jnp.where(valid[:, :, None, None, :], logits, NEG)
    p = jax.nn.softmax(logits, axis=-1)
    o = jnp.einsum('bqngk,bqknd->bqngd', p, vg.astype(jnp.float32))
    return o.reshape(B, Q, ATTN_WIDTH).astype(q.dtype)

def dsa_prompt(q, k, v, qi, ki, wi):
    B, T = q.shape[:2]
    nb = T // Q_BLOCK
    topk = min(TOPK_MAX, T // 4)
    take = jax.vmap(lambda rows, ids: rows[ids])

    def to_blocks(a):
        return jnp.moveaxis(a.reshape((B, nb, Q_BLOCK) + a.shape[2:]), 1, 0)

    def one_block(args):
        qb, qib, wib, start = args
        q_pos = start + jnp.arange(Q_BLOCK, dtype=jnp.int32)
        idx, valid = indexer_topk(qib, wib, ki, q_pos, topk)
        return sparse_attend(qb, take(k, idx), take(v, idx), valid)

    starts = jnp.arange(nb, dtype=jnp.int32) * Q_BLOCK
    out = lax.map(one_block, (to_blocks(q), to_blocks(qi), to_blocks(wi), starts))
    return jnp.moveaxis(out, 0, 1).reshape(B, T, ATTN_WIDTH)

def gather_paged(pool, new, idx, page_table):
    DB = idx.shape[0]
    n_pages = page_table.shape[1]
    past_len = n_pages * PAGE_SIZE
    page = jnp.minimum(idx // PAGE_SIZE, n_pages - 1)
    phys = jnp.take_along_axis(page_table, page.reshape(DB, -1), axis=1).reshape(idx.shape)
    past_rows = pool[phys, idx % PAGE_SIZE]
    new_rows = jax.vmap(lambda rows, ids: rows[ids])(new, jnp.clip(idx - past_len, 0, new.shape[1] - 1))
    in_past = (idx < past_len).reshape(idx.shape + (1,) * (past_rows.ndim - 3))
    return jnp.where(in_past, past_rows, new_rows)

def s5_scan(u, h0_re, h0_im, lam_re, lam_im, log_dt, b_re, b_im, c_re, c_im, d_skip):
    B, T, _ = u.shape
    uf = u.astype(jnp.float32).reshape(B, T, N_SSM_GROUPS, SSM_GROUP)
    dt = jnp.exp(log_dt.astype(jnp.float32))[:, None]
    lr, li = lam_re.astype(jnp.float32), lam_im.astype(jnp.float32)
    mag = jnp.exp(lr * dt)
    ar, ai = mag * jnp.cos(li * dt), mag * jnp.sin(li * dt)
    den = lr * lr + li * li
    cr = ((ar - 1.0) * lr + ai * li) / den
    ci = (ai * lr - (ar - 1.0) * li) / den
    br, bi = b_re.astype(jnp.float32), b_im.astype(jnp.float32)
    bbr = cr[..., None] * br - ci[..., None] * bi
    bbi = cr[..., None] * bi + ci[..., None] * br
    bu_re = jnp.einsum('gpc,btgc->btgp', bbr, uf)
    bu_im = jnp.einsum('gpc,btgc->btgp', bbi, uf)
    h0r, h0i = h0_re.astype(jnp.float32), h0_im.astype(jnp.float32)
    bu_re = bu_re.at[:, 0].add(ar * h0r - ai * h0i)
    bu_im = bu_im.at[:, 0].add(ar * h0i + ai * h0r)
    a_re = jnp.broadcast_to(ar, (1, T, N_SSM_GROUPS, SSM_STATE))
    a_im = jnp.broadcast_to(ai, (1, T, N_SSM_GROUPS, SSM_STATE))

    def combine(e1, e2):
        a1r, a1i, b1r, b1i = e1
        a2r, a2i, b2r, b2i = e2
        return (a1r * a2r - a1i * a2i, a1r * a2i + a1i * a2r,
                a2r * b1r - a2i * b1i + b2r, a2r * b1i + a2i * b1r + b2i)

    _, _, hr, hi = lax.associative_scan(combine, (a_re, a_im, bu_re, bu_im), axis=1)
    y = (jnp.einsum('gcp,btgp->btgc', c_re.astype(jnp.float32), hr)
         - jnp.einsum('gcp,btgp->btgc', c_im.astype(jnp.float32), hi)
         + d_skip.astype(jnp.float32).reshape(N_SSM_GROUPS, SSM_GROUP) * uf)
    return y.reshape(B, T, SSM_WIDTH), hr[:, -1], hi[:, -1]

def glu_out(y, w_glu, b_glu, dtype):
    z = jax.nn.gelu(y)
    gate = jax.nn.sigmoid(z @ w_glu.astype(jnp.float32) + b_glu.astype(jnp.float32))
    return (z * gate).astype(dtype)

def residual_block(x, a_o, s_o, w_out, g_post, g_ffn_pre, w_up, w_down, g_ffn_post):
    mix = jnp.concatenate([a_o, s_o], axis=-1) @ w_out
    x = x + rmsnorm(mix, g_post)
    hdn = jnp.square(jax.nn.relu(rmsnorm(x, g_ffn_pre) @ w_up))
    return x + rmsnorm(hdn @ w_down, g_ffn_post)

def setup_inputs(seed: int = 0) -> dict:
    key = jax.random.key(seed)
    ks = jax.random.split(key, 32)
    n_pages = PAST_LEN // PAGE_SIZE
    n_used = DEC_BATCH * n_pages
    n_phys = n_used + max(1, n_used // 4)
    nrm = jax.random.normal
    f32 = jnp.float32
    page_table = jax.random.permutation(ks[0], n_phys)[:n_used].reshape(DEC_BATCH, n_pages).astype(jnp.int32)
    log_dt = jax.random.uniform(ks[1], (DEPTH, N_SSM_GROUPS), f32, math.log(DT_MIN), math.log(DT_MAX))
    lam_im = (jnp.pi * jnp.arange(SSM_STATE, dtype=f32))[None, None, :] + 0.01 * nrm(ks[2], (DEPTH, N_SSM_GROUPS, SSM_STATE), f32)
    return {
        'x_prompt': nrm(ks[3], (BATCH, SEQ, D_MODEL), f32),
        'x_sample': nrm(ks[4], (DEC_BATCH, DEC_SEQ, D_MODEL), f32),
        'cache_k': nrm(ks[5], (DEPTH, n_phys, PAGE_SIZE, N_KV_HEADS, HEAD_DIM), f32),
        'cache_v': nrm(ks[6], (DEPTH, n_phys, PAGE_SIZE, N_KV_HEADS, HEAD_DIM), f32),
        'cache_kidx': nrm(ks[7], (DEPTH, n_phys, PAGE_SIZE, IDX_DIM), f32),
        'state_ssm_re': 0.5 * nrm(ks[8], (DEPTH, DEC_BATCH, N_SSM_GROUPS, SSM_STATE), f32),
        'state_ssm_im': 0.5 * nrm(ks[9], (DEPTH, DEC_BATCH, N_SSM_GROUPS, SSM_STATE), f32),
        'page_table': page_table,
        'norm_mix_pre': 1.0 + 0.05 * nrm(ks[10], (DEPTH, D_MODEL), f32),
        'w_in': nrm(ks[11], (DEPTH, D_MODEL, IN_WIDTH), f32) * D_MODEL ** -0.5,
        'lambda_re': -0.5 + 0.01 * nrm(ks[12], (DEPTH, N_SSM_GROUPS, SSM_STATE), f32),
        'lambda_im': lam_im,
        'log_dt': log_dt,
        'b_re': nrm(ks[13], (DEPTH, N_SSM_GROUPS, SSM_STATE, SSM_GROUP), f32) * (2 * SSM_GROUP) ** -0.5,
        'b_im': nrm(ks[14], (DEPTH, N_SSM_GROUPS, SSM_STATE, SSM_GROUP), f32) * (2 * SSM_GROUP) ** -0.5,
        'c_re': nrm(ks[15], (DEPTH, N_SSM_GROUPS, SSM_GROUP, SSM_STATE), f32) * (2 * SSM_STATE) ** -0.5,
        'c_im': nrm(ks[16], (DEPTH, N_SSM_GROUPS, SSM_GROUP, SSM_STATE), f32) * (2 * SSM_STATE) ** -0.5,
        'd_skip': nrm(ks[17], (DEPTH, SSM_WIDTH), f32),
        'w_glu': nrm(ks[18], (DEPTH, SSM_WIDTH, SSM_WIDTH), f32) * SSM_WIDTH ** -0.5,
        'b_glu': 0.01 * nrm(ks[19], (DEPTH, SSM_WIDTH), f32),
        'w_out': nrm(ks[20], (DEPTH, ATTN_WIDTH + SSM_WIDTH, D_MODEL), f32) * (ATTN_WIDTH + SSM_WIDTH) ** -0.5,
        'norm_mix_post': 1.0 + 0.05 * nrm(ks[21], (DEPTH, D_MODEL), f32),
        'norm_ffn_pre': 1.0 + 0.05 * nrm(ks[22], (DEPTH, D_MODEL), f32),
        'w_up': nrm(ks[23], (DEPTH, D_MODEL, D_FF), f32) * D_MODEL ** -0.5,
        'w_down': nrm(ks[24], (DEPTH, D_FF, D_MODEL), f32) * D_FF ** -0.5,
        'norm_ffn_post': 1.0 + 0.05 * nrm(ks[25], (DEPTH, D_MODEL), f32),
    }

def reference(x_prompt, x_sample, cache_k, cache_v, cache_kidx, state_ssm_re, state_ssm_im, page_table,
              norm_mix_pre, w_in, lambda_re, lambda_im, log_dt, b_re, b_im, c_re, c_im, d_skip,
              w_glu, b_glu, w_out, norm_mix_post, norm_ffn_pre, w_up, w_down, norm_ffn_post):
    past_len = page_table.shape[1] * PAGE_SIZE
    dec_b, dec_t = x_sample.shape[0], x_sample.shape[1]
    pos_p = jnp.arange(x_prompt.shape[1], dtype=jnp.int32)
    pos_s = past_len + jnp.arange(dec_t, dtype=jnp.int32)
    topk_s = min(TOPK_MAX, (past_len + dec_t) // 4)
    hp, hs = x_prompt, x_sample
    kp_l, vp_l, kip_l, srp_l, sip_l = [], [], [], [], []
    ks_l, vs_l, kis_l, srs_l, sis_l = [], [], [], [], []
    for l in range(DEPTH):
        ssm_w = (lambda_re[l], lambda_im[l], log_dt[l], b_re[l], b_im[l], c_re[l], c_im[l], d_skip[l])
        tail = (w_out[l], norm_mix_post[l], norm_ffn_pre[l], w_up[l], w_down[l], norm_ffn_post[l])
        q, k, v, qi, ki, wi, u = mixer_inputs(hp, pos_p, norm_mix_pre[l], w_in[l])
        a_o = dsa_prompt(q, k, v, qi, ki, wi)
        h0 = jnp.zeros((hp.shape[0], N_SSM_GROUPS, SSM_STATE), jnp.float32)
        y_ssm, hr, hi = s5_scan(u, h0, h0, *ssm_w)
        s_o = glu_out(y_ssm, w_glu[l], b_glu[l], hp.dtype)
        hp = residual_block(hp, a_o, s_o, *tail)
        kp_l.append(k); vp_l.append(v); kip_l.append(ki); srp_l.append(hr); sip_l.append(hi)
        q, k, v, qi, ki, wi, u = mixer_inputs(hs, pos_s, norm_mix_pre[l], w_in[l])
        ki_past = cache_kidx[l][page_table].reshape(dec_b, past_len, IDX_DIM)
        ki_all = jnp.concatenate([ki_past, ki.astype(ki_past.dtype)], axis=1)
        idx, valid = indexer_topk(qi, wi, ki_all, pos_s, topk_s)
        kg = gather_paged(cache_k[l], k, idx, page_table)
        vg = gather_paged(cache_v[l], v, idx, page_table)
        a_o = sparse_attend(q, kg, vg, valid)
        y_ssm, hr, hi = s5_scan(u, state_ssm_re[l], state_ssm_im[l], *ssm_w)
        s_o = glu_out(y_ssm, w_glu[l], b_glu[l], hs.dtype)
        hs = residual_block(hs, a_o, s_o, *tail)
        ks_l.append(k); vs_l.append(v); kis_l.append(ki); srs_l.append(hr); sis_l.append(hi)
    return (hp, hs,
            jnp.stack(kp_l), jnp.stack(vp_l), jnp.stack(kip_l), jnp.stack(srp_l), jnp.stack(sip_l),
            jnp.stack(ks_l), jnp.stack(vs_l), jnp.stack(kis_l), jnp.stack(srs_l), jnp.stack(sis_l))


_drawn_inputs = setup_inputs


def setup_inputs(seed=0):
    import zlib

    import numpy as np

    out = dict(_drawn_inputs(seed))
    spreads = {}
    factors = {'lambda_re': 4.195, 'b_glu': 8.0}
    for name, (base, spread) in spreads.items():
        noise = np.random.default_rng([zlib.crc32(name.encode()), seed]).standard_normal(out[name].shape)
        drawn = base * np.exp(spread * noise) if base else spread * noise
        out[name] = __import__('jax').numpy.asarray(drawn.astype(out[name].dtype))
    for name, factor in factors.items():
        out[name] = (out[name] * factor).astype(out[name].dtype)
    return out
```

```python
from contextlib import ExitStack
import numpy as np
import concourse.bass as bass
from concourse import mybir
from concourse.alu_op_type import AluOpType as ALU

ACT = mybir.ActivationFunctionType
AX = mybir.AxisListType
F32 = mybir.dt.float32
F32R = mybir.dt.float32r
I32 = mybir.dt.int32

P = 128
D = 1024
KD = D // P
SEQ = 2048
NPT = SEQ // P
NT = NPT + 1
NTOK = NT * P
DECB, DECT = 8, 8
NS = DECB * DECT
PAST = 4096
PAGE = 128
NPAGE = PAST // PAGE
HD = 64
NH, NKV, NIH = 8, 2, 4
QPK = NH // NKV
TOPK = 256
OFF_K, OFF_V, OFF_QI, OFF_KI, OFF_WI, OFF_U, IN_W = 512, 640, 768, 1024, 1088, 1092, 1604
BANKS = ((0, 512), (512, 768), (768, 1092), (1092, 1604))
G, GC, SS = 32, 16, 64
GP = G // 2
CH = 8
NCH = NTOK // CH
NCP = SEQ // CH
NCU = NCP + DECB
DFF = 4096
EPS = 1e-6
NEG = -1e30
TAKEN = -3e38


def inverse_root(dve, y, mean, root, tmp, step, done):
    dve.reciprocal(y, root).then_inc(step, 1)
    dve.wait_ge(step, done + 1)
    dve.tensor_tensor(tmp, y, y, ALU.mult).then_inc(step, 1)
    dve.wait_ge(step, done + 2)
    dve.tensor_tensor(tmp, tmp, mean, ALU.mult).then_inc(step, 1)
    dve.wait_ge(step, done + 3)
    dve.tensor_scalar(tmp, tmp, -0.5, 1.5, ALU.mult, ALU.add).then_inc(step, 1)
    dve.wait_ge(step, done + 4)
    return dve.tensor_tensor(y, y, tmp, ALU.mult)


def project_inputs(nc, A, R, ident):
    with ExitStack() as ctx:
        sb = lambda n, s, d=F32: ctx.enter_context(nc.sbuf_tensor(n + "_sb1", s, d))
        sem = lambda n: ctx.enter_context(nc.semaphore(n))
        w_raw = sb("w_raw", [P, 2, IN_W])
        w_hi = sb("w_hi", [P, KD, IN_W], F32R)
        w_lo = sb("w_lo", [P, KD, IN_W], F32R)
        gpre = sb("gpre", [P, KD])
        x_tok = sb("x_tok", [P, 2, D])
        x_sq = sb("x_sq", [P, D])
        xT = sb("xT", [P, 2, KD, P])
        xT_hi = sb("xT_hi", [P, 2, KD, P], F32R)
        xT_lo = sb("xT_lo", [P, 2, KD, P], F32R)
        cs = sb("cs", [P, 2, 2 * HD])
        ssum = sb("ssum", [P, NT])
        rstd = sb("rstd", [P, NT])
        mean_sq = sb("mean_sq", [P, NT])
        rms = sb("rms", [P, NT])
        newton_s = sb("newton_s", [P, 1])
        newton = newton_s[:]
        pr = w_raw
        qT = sb("qT", [P, 2, 4, P])
        qiT = sb("qiT", [P, 2, 2, P])
        t1 = sb("t1", [P, 10, HD])
        t2 = sb("t2", [P, 10, HD])
        t3 = sb("t3", [P, 5, HD])
        t4 = sb("t4", [P, 5, HD])
        qk = sb("qk", [P, 2, 10, HD])
        qi = sb("qi", [P, 2, 6, HD])
        pp = [ctx.enter_context(nc.psum_tensor(f"pp{j}", [P, 512], F32)) for j in range(4)]
        pt = [ctx.enter_context(nc.psum_tensor(f"pt{j}", [P, 4, P], F32)) for j in range(2)]
        w_ld = [sem(f"w_ld{i}") for i in range(2)]
        w_scaled, w_hi_ok, w_lo_ok = sem("w_scaled"), sem("w_hi_ok"), sem("w_lo_ok")
        g_ld = sem("g_ld")
        x_ld = [sem(f"x_ld{i}") for i in range(2)]
        sum_ok, rs_mid, rs_ok = sem("sum_ok"), sem("rs_mid"), sem("rs_ok")
        mean_ok, root_ok = sem("mean_ok"), sem("root_ok")
        xhi_ok, xlo_ok = sem("xhi_ok"), sem("xlo_ok")
        proj_ok, pr_ok = sem("proj_ok"), sem("pr_ok")
        ropeq, ropei = sem("ropeq"), sem("ropei")
        tr_ok, te_ok = sem("tr_ok"), sem("te_ok")
        out_ok = [sem(f"out_ok{i}") for i in range(2)]
        copied = sem("copied")
        stored = sem("stored")
        with nc.Block() as block:
            def store_tile(sp, t):
                s = t % 2
                sp.wait_ge(ropei, 5 * t + 5)
                sp.wait_ge(ropeq, 4 * t + 4)
                m, ko, vo, io, a = (P, "k_p", "v_p", "ki_p", t * P) if t < NPT else (NS, "k_s", "v_s", "ki_s", 0)
                sp.dma_start(A[ko][a:a + m, :], qk[0:m, s, 8:10, :]).then_inc(out_ok[s], 16)
                sp.dma_start(A[io][a:a + m, :], qi[0:m, s, 4, :]).then_inc(out_ok[s], 16)
                sp.wait_ge(pr_ok, 4 * t + 4)
                sp.dma_start(A[vo][a:a + m, :], pr[0:m, s, OFF_V:OFF_QI]).then_inc(out_ok[s], 16)
                sp.dma_start(A["u_d"][t * P:(t + 1) * P, :], pr[:, s, OFF_U:IN_W]).then_inc(out_ok[s], 16)
                sp.wait_ge(te_ok, 4 * t + 4)
                sp.dma_start(A["q_d"][t], qT[:, s]).then_inc(out_ok[s], 16)
                sp.dma_start(A["qi_d"][t], qiT[:, s]).then_inc(out_ok[s], 16)

            def load_tile(sp, t):
                s = slice(t * P, (t + 1) * P)
                sp.dma_start(x_tok[:, t % 2, :], A["x_all"][s, :]).then_inc(x_ld[t % 2], 16)
                sp.dma_start(xT[:, t % 2, :, :], A["xT_all"][t]).then_inc(x_ld[t % 2], 16)
                sp.dma_start(cs[:, t % 2, :], A["rope"][s, :]).then_inc(x_ld[t % 2], 16)

            @block.sync
            def _(sp):
                sp.dma_start(gpre[:], A["g_pre"]).then_inc(g_ld, 16)
                for k in range(KD):
                    if k >= 2:
                        sp.wait_ge(w_lo_ok, k - 1)
                    sp.dma_start(w_raw[:, k % 2, :], A["w_in"][k * P:(k + 1) * P, :]).then_inc(w_ld[k % 2], 16)
                    if k < 2:
                        load_tile(sp, k)
                for t in range(2, NT):
                    sp.wait_ge(xlo_ok, t - 1)
                    sp.wait_ge(sum_ok, t - 1)
                    sp.wait_ge(ropeq, 4 * (t - 1))
                    sp.wait_ge(ropei, 5 * (t - 1))
                    load_tile(sp, t)
                    store_tile(sp, t - 2)
                store_tile(sp, NT - 2)
                store_tile(sp, NT - 1)
                for i in range(2):
                    sp.wait_ge(out_ok[i], 96 * ((NT - i + 1) // 2))
                sp.dma_start(R["qk_s"][:], qk[0:NS, (NT - 1) % 2]).then_inc(stored, 16)
                sp.dma_start(R["qi_s"][:], qi[0:NS, (NT - 1) % 2]).then_inc(stored, 16)
                sp.wait_ge(stored, 32)

            @block.scalar
            def _(act):
                def square_and_high(t):
                    act.wait_ge(x_ld[t % 2], 48 * (t // 2 + 1))
                    if t:
                        act.wait_ge(sum_ok, t)
                    act.activation(x_sq[:], x_tok[:, t % 2, :], ACT.Square, accum_out=ssum[:, t:t + 1]).then_inc(sum_ok, 1)
                    if t >= 2:
                        act.wait_ge(proj_ok, 4 * (t - 1))
                    act.activation(xT_hi[:, t % 2], xT[:, t % 2], ACT.Copy).then_inc(xhi_ok, 1)
                    act.wait_ge(mean_ok, t + 1)
                    act.activation(rms[:, t:t + 1], mean_sq[:, t:t + 1], ACT.Sqrt).then_inc(root_ok, 1)

                def evacuate(t):
                    act.wait_ge(rs_ok, t + 1)
                    if t >= 2:
                        act.wait_ge(copied, t - 1)
                        act.wait_ge(ropeq, 4 * (t - 1))
                        act.wait_ge(ropei, 5 * (t - 1))
                        act.wait_ge(tr_ok, 2 * (t - 1))
                        act.wait_ge(out_ok[t % 2], 96 * (t // 2))
                    for j, (a, b) in enumerate(BANKS):
                        act.wait_ge(proj_ok, 4 * t + j + 1)
                        act.activation(pr[:, t % 2, a:b], pp[j][:, 0:b - a], ACT.Copy,
                                       scale=rstd[:, t:t + 1]).then_inc(pr_ok, 1)

                def keep_transposes(t):
                    act.wait_ge(tr_ok, 2 * t + 1)
                    if t >= 2:
                        act.wait_ge(out_ok[t % 2], 96 * (t // 2))
                    act.activation(qT[:, t % 2], pt[0][:], ACT.Copy).then_inc(te_ok, 1)
                    act.wait_ge(tr_ok, 2 * t + 2)
                    act.activation(R["kT"][:, t * P:(t + 1) * P], pt[1][:, 0, :], ACT.Copy).then_inc(te_ok, 1)
                    act.activation(qiT[:, t % 2], pt[1][:, 1:3, :], ACT.Copy).then_inc(te_ok, 1)
                    act.activation(R["kiT"][:, t * P:(t + 1) * P], pt[1][:, 3, :], ACT.Copy).then_inc(te_ok, 1)

                for k in range(KD):
                    act.wait_ge(w_scaled, k + 1)
                    act.activation(w_hi[:, k, :], w_raw[:, k % 2, :], ACT.Copy).then_inc(w_hi_ok, 1)
                square_and_high(0)
                for t in range(NT):
                    if t + 1 < NT:
                        square_and_high(t + 1)
                    evacuate(t)
                    if t:
                        keep_transposes(t - 1)
                keep_transposes(NT - 1)

            @block.vector
            def _(dve):
                dve.wait_ge(g_ld, 16)
                for k in range(KD):
                    dve.wait_ge(w_ld[k % 2], 16 * (k // 2 + 1))
                    dve.tensor_scalar(w_raw[:, k % 2, :], w_raw[:, k % 2, :], gpre[:, k:k + 1], None,
                                      ALU.mult).then_inc(w_scaled, 1)
                    dve.wait_ge(w_hi_ok, k + 1)
                    dve.tensor_tensor(w_lo[:, k, :], w_raw[:, k % 2, :], w_hi[:, k, :].bitcast(F32),
                                      ALU.subtract).then_inc(w_lo_ok, 1)

                def low_part(t):
                    dve.wait_ge(xhi_ok, t + 1)
                    dve.tensor_tensor(xT_lo[:, t % 2], xT[:, t % 2], xT_hi[:, t % 2].bitcast(F32),
                                      ALU.subtract).then_inc(xlo_ok, 1)
                    mean, root, y = mean_sq[:, t:t + 1], rms[:, t:t + 1], rstd[:, t:t + 1]
                    dve.wait_ge(sum_ok, t + 1)
                    dve.tensor_scalar(mean, ssum[:, t:t + 1], 1.0 / D, EPS, ALU.mult, ALU.add).then_inc(mean_ok, 1)
                    dve.wait_ge(root_ok, t + 1)
                    inverse_root(dve, y, mean, root, newton, rs_mid, 4 * t).then_inc(rs_ok, 1)

                low_part(0)
                for t in range(NT):
                    if t + 1 < NT:
                        low_part(t + 1)
                    s = t % 2
                    dve.wait_ge(pr_ok, 4 * t + 2)
                    x = pr[:, s, 0:10 * HD].rearrange("p (h d) -> p h d", d=HD)
                    cos = cs[:, s, None, 0:HD].to_broadcast([P, 10, HD])
                    sin = cs[:, s, None, HD:2 * HD].to_broadcast([P, 10, HD])
                    if t:
                        dve.wait_ge(ropeq, 4 * t)
                    dve.tensor_tensor(t1[:], x, cos, ALU.mult).then_inc(ropeq, 1)
                    dve.tensor_tensor(t2[:, :, 0:32], x[:, :, 32:64], sin[:, :, 0:32], ALU.mult).then_inc(ropeq, 1)
                    dve.tensor_tensor(t2[:, :, 32:64], x[:, :, 0:32], sin[:, :, 32:64], ALU.mult).then_inc(ropeq, 1)
                    dve.tensor_copy(R["V"][:, t, :], pr[:, s, OFF_V:OFF_QI])
                    dve.wait_ge(pr_ok, 4 * t + 3)
                    dve.tensor_copy(R["wi"][:, t, :], pr[:, s, OFF_WI:OFF_U]).then_inc(copied, 1)
                    dve.wait_ge(ropeq, 4 * t + 3)
                    if t >= 2:
                        dve.wait_ge(tr_ok, 2 * (t - 1))
                        dve.wait_ge(out_ok[s], 96 * (t // 2))
                    dve.tensor_tensor(qk[:, s], t1[:], t2[:], ALU.add).then_inc(ropeq, 1)

            @block.gpsimd
            def _(pool):
                for t in range(NT):
                    s = t % 2
                    pool.wait_ge(pr_ok, 4 * t + 3)
                    x = pr[:, s, OFF_QI:OFF_WI].rearrange("p (h d) -> p h d", d=HD)
                    cos = cs[:, s, None, 0:HD].to_broadcast([P, 5, HD])
                    sin = cs[:, s, None, HD:2 * HD].to_broadcast([P, 5, HD])
                    if t:
                        pool.wait_ge(ropei, 5 * t)
                    pool.tensor_tensor(t3[:], x, cos, ALU.mult).then_inc(ropei, 1)
                    pool.tensor_tensor(t4[:, :, 0:32], x[:, :, 32:64], sin[:, :, 0:32], ALU.mult).then_inc(ropei, 1)
                    pool.tensor_tensor(t4[:, :, 32:64], x[:, :, 0:32], sin[:, :, 32:64], ALU.mult).then_inc(ropei, 1)
                    pool.wait_ge(ropei, 5 * t + 3)
                    if t >= 2:
                        pool.wait_ge(tr_ok, 2 * (t - 1))
                        pool.wait_ge(out_ok[s], 96 * (t // 2))
                    pool.tensor_tensor(qi[:, s, 0:5], t3[:], t4[:], ALU.add).then_inc(ropei, 1)
                    pool.tensor_tensor(qi[:, s, 5], t3[:, 4], t4[:, 4], ALU.add).then_inc(ropei, 1)

            @block.tensor
            def _(pe):
                def project(t):
                    pe.wait_ge(xlo_ok, t + 1)
                    for j, (a, b) in enumerate(BANKS):
                        if t:
                            pe.wait_ge(pr_ok, 4 * (t - 1) + j + 1)
                        n = 0
                        for k in range(KD):
                            if t == 0 and j == 0:
                                pe.wait_ge(w_lo_ok, k + 1)
                            for x, w in ((xT_hi, w_hi), (xT_hi, w_lo), (xT_lo, w_hi)):
                                mm = pe.matmul(pp[j][:, 0:b - a], x[:, t % 2, k, :], w[:, k, a:b],
                                               start=n == 0, stop=n == 3 * KD - 1)
                                n += 1
                        mm.then_inc(proj_ok, 1)

                def turn(t):
                    s = t % 2
                    pe.wait_ge(ropeq, 4 * t + 4)
                    if t:
                        pe.wait_ge(te_ok, 4 * t)
                    for a in range(4):
                        mm = pe.transpose(pt[0][:, a, :], qk[:, s, 2 * a:2 * a + 2, :], ident[:])
                    mm.then_inc(tr_ok, 1)
                    pe.transpose(pt[1][:, 0, :], qk[:, s, 8:10, :], ident[:])
                    pe.wait_ge(ropei, 5 * t + 5)
                    for a in range(3):
                        mm = pe.transpose(pt[1][:, 1 + a, :], qi[:, s, 2 * a:2 * a + 2, :], ident[:])
                    mm.then_inc(tr_ok, 1)

                for t in range(NT):
                    project(t)
                    if t:
                        turn(t - 1)
                turn(NT - 1)




class Count:

    def __init__(self, eng, sem):
        self.eng, self.sem, self.n = eng, sem, 0

    def up(self, ins):
        ins.then_inc(self.sem, 1)
        self.n += 1

    def wait(self):
        self.eng.wait_ge(self.sem, self.n)

    def step(self, ins):
        self.up(ins)
        self.wait()


def complex_product(dve, c, o_r, o_i, a_r, a_i, b_r, b_i, x, y):
    c.up(dve.tensor_tensor(x, a_r, b_r, ALU.mult))
    c.up(dve.tensor_tensor(y, a_i, b_i, ALU.mult))
    c.wait()
    c.step(dve.tensor_tensor(y, x, y, ALU.subtract))
    c.step(dve.tensor_tensor(x, a_r, b_i, ALU.mult))
    c.step(dve.tensor_tensor(o_i, a_i, b_r, ALU.mult))
    c.up(dve.tensor_tensor(o_i, o_i, x, ALU.add))
    c.up(dve.tensor_copy(o_r, y))
    c.wait()


def state_space(nc, A, R, ident):
    PI2_HI = 6.28125
    PI2_LO = float(2 * np.pi - PI2_HI)
    ROUND = 1.5 * 2.0 ** 23
    NSC = 2 * DECB
    CT = (P, P, NSC)
    base = lambda t: 16 + 40 * t
    U8, W, Y, ZT, GL = 8, 16, 24, 32, 40
    with ExitStack() as ctx:
        sb = lambda n, s, d=F32: ctx.enter_context(nc.sbuf_tensor(n + "_sb2", s, d))
        sem = lambda n: ctx.enter_context(nc.semaphore(n))
        lamr, lami, ldt = sb("lamr", [P, GP]), sb("lami", [P, GP]), sb("ldt", [P, GP])
        br, bi = sb("br", [P, GP, GC]), sb("bi", [P, GP, GC])
        dsk = sb("dsk", [GC, G])
        bglu = sb("bglu", [P, 4])
        wglu = sb("wglu", [P, 4, 512])
        U = sb("U", [P, CH, 512])
        Ur = sb("Ur", [P, G * CH * GC])
        u8 = sb("u8", [P, G, P])
        wr, wi = sb("wr", [P, GP, P]), sb("wi_s", [P, GP, P])
        Hr, Hi = sb("Hr", [P, GP, P + 1]), sb("Hi", [P, GP, P + 1])
        zT = sb("zT", [P, 4, P, CH])
        Tr, Ti = sb("Tr", [P, GP, P]), sb("Ti", [P, GP, P])
        MT = sb("MT", [P, G, CH * GC])
        BTr, BTi = sb("BTr", [P, GP, P]), sb("BTi", [P, GP, P])
        CAr, CAi = sb("CAr", [P, GP, CH + 1, GC]), sb("CAi", [P, GP, CH + 1, GC])
        BAr = Ur[:, 0:GP * P].rearrange("p (g j c) -> p g j c", g=GP, c=GC)
        BAi = Ur[:, GP * P:2 * GP * P].rearrange("p (g j c) -> p g j c", g=GP, c=GC)
        KT = U[:].rearrange("p j c -> p (j c)")[0:GC, :].rearrange("p (g m) -> p g m", g=G)
        Urv = Ur[:].rearrange("p (g j c) -> p g j c", g=G, c=GC)
        Urj = Ur[:].rearrange("p (g m) -> p g m", g=G)
        dv = Ur[:].rearrange("p (b g n) -> p b g n", b=2, g=GP)
        pv = zT[:].rearrange("p f n t -> p (f n t)").rearrange("p (b g n) -> p b g n", b=2, g=GP)
        so = Ur[:].rearrange("p (f n t) -> p f n t", f=4, t=CH)
        eyed = wr[0:GC].rearrange("p g n -> p (g n)")[:, 0:G * GC].rearrange("p (g c) -> p g c", g=G)
        sm = sb("sm", [P, 20, GP])
        gate = sb("gate", [P, 2, 512])
        h0r, h0i = sb("h0r", [P, GP, NSC]), sb("h0i", [P, GP, NSC])
        fin_p, fin_s = sb("fin_p", [P, 2, GP]), sb("fin_s", [P, 2, GP, DECB])
        ps = [ctx.enter_context(nc.psum_tensor(f"ps{j}", [P, 512], F32)) for j in range(8)]
        ld, u_ld = sem("ld"), [sem("u_ld0"), sem("u_ld1"), sem("u_ld2")]
        bank_full, bank_free = sem("bank_full"), sem("bank_free")
        dt_ok, decay_in, angles_ok, decay_ok, trig_ok = (sem(x) for x in ("dt_ok", "decay_in", "angles_ok", "decay_ok", "trig_ok"))
        ba_ok, ca_ok, mt_zero, kt_ok, mt_ok = (sem(x) for x in ("ba_ok", "ca_ok", "mt_zero", "kt_ok", "mt_ok"))
        tab_ok, h00_ok = sem("tab_ok"), sem("h00_ok")
        ur_ok, vi_ok, scan_ok, hr_ok, hi_ok, carry_ok = (sem(x) for x in ("ur_ok", "vi_ok", "scan_ok", "hr_ok", "hi_ok", "carry_ok"))
        so_ok, so_st, fin_ok, fin_st = (sem(x) for x in ("so_ok", "so_st", "fin_ok", "fin_st"))
        dve_own, pool_own = sem("dve_own"), sem("pool_own")
        NLD = 12
        NGL = (8, 8, 4)
        ngl = lambda t: sum(NGL[:t])
        DT, MAG, TH, K1, K2, RS, RC, SIN, COS, AR, AI, DEN, CR, CI, X, Y_, W_, R8, PR, PI_ = range(20)
        S = lambda i: sm[:, i, :]
        of_bank = lambda q: slice(8 * (q % 4) + q // 4, 8 * (q % 4) + 8, 2)
        with nc.Block() as block:
            def store_gated(sp, t):
                sp.wait_ge(so_ok, ngl(t + 1))
                k = -(-CT[t] * CH // P)
                for f in range(4):
                    sp.dma_start(A["so_d"][8 * t:8 * t + k, :, f, :].rearrange("s p q -> p s q"),
                                 so[:, f, 0:CT[t], :].rearrange("p n t -> p (n t)").rearrange("p (s q) -> p s q", q=P)).then_inc(so_st, 16)

            @block.sync
            def _(sp):
                for dst, name in ((lamr, "lam_re"), (lami, "lam_im"), (ldt, "log_dt"), (br, "b_re"), (bi, "b_im"),
                                  (dsk, "d_skip"), (bglu, "b_glu"), (wglu, "w_glu"), (h0r, "h0_re"), (h0i, "h0_im")):
                    sp.dma_start(dst[:], A[name]).then_inc(ld, 16)
                sp.dma_start(CAr[:, :, 0, :], A["c_re"]).then_inc(ld, 16)
                sp.dma_start(CAi[:, :, 0, :], A["c_im"]).then_inc(ld, 16)
                sp.wait_ge(kt_ok, 1)
                sp.wait_ge(mt_zero, 1)
                for j in range(CH):
                    sp.dma_start(MT[j * GC:(j + 1) * GC, :, j * GC:], KT[:, :, 0:(CH - j) * GC]).then_inc(mt_ok, 16)
                sp.wait_ge(mt_ok, 16 * CH)
                for t, n in enumerate(CT):
                    if t:
                        sp.wait_ge(bank_full, base(t - 1) + ZT)
                    sp.dma_start(U[0:n], A["u_d"][t * P * CH:t * P * CH + n * CH, :].rearrange("(n j) c -> n j c", j=CH)).then_inc(u_ld[t], 16)
                    if t:
                        store_gated(sp, t - 1)
                store_gated(sp, 2)
                sp.wait_ge(fin_ok, 2)
                for k, name in ((0, "hp_re"), (1, "hp_im")):
                    sp.dma_start(A[name], fin_p[:, k]).then_inc(fin_st, 16)
                for k, name in ((0, "hs_re"), (1, "hs_im")):
                    sp.dma_start(A[name], fin_s[:, k]).then_inc(fin_st, 16)
                sp.wait_ge(fin_st, 64)
                sp.wait_ge(so_st, 16 * (4 + 4 + 4))

            @block.scalar
            def _(act):
                act.wait_ge(ld, 16 * NLD)
                act.activation(S(DT), ldt[:], ACT.Exp).then_inc(dt_ok, 1)
                act.wait_ge(decay_in, 1)
                act.activation(S(MAG), S(X), ACT.Exp).then_inc(decay_ok, 1)
                act.wait_ge(angles_ok, 1)
                act.activation(S(SIN), S(RS), ACT.Sin).then_inc(trig_ok, 1)
                act.activation(S(COS), S(RC), ACT.Sin).then_inc(trig_ok, 1)
                full = [0]

                def empty(out, fn, func=ACT.Copy, **kw):
                    i = full[0]
                    full[0] += 1
                    act.wait_ge(bank_full, i + 1)
                    act.activation(out, fn(ps[i % 8]), func, **kw).then_inc(bank_free, 1)

                four = lambda n: lambda b: b[:, :].rearrange("p (g m) -> p g m", g=4)[:, :, 0:n]
                for BT in (BTr, BTi):
                    for q in range(4):
                        empty(BT[:, 4 * q:4 * q + 4, :], four(P))
                for q in range(8):
                    empty(KT[:, of_bank(q), :], lambda b: b[0:GC, :].rearrange("p (g m) -> p g m", g=4))
                act.wait_ge(tab_ok, 1)
                for t, n in enumerate(CT):
                    for q in range(8):
                        empty(u8[:, 4 * q:4 * q + 4, 0:n], four(n))
                    if t:
                        act.wait_ge(hr_ok, t)
                        act.wait_ge(hi_ok, t)
                    for w in (wr, wi):
                        for q in range(4):
                            empty(w[:, 4 * q:4 * q + 4, 0:n], four(n))
                    for q in range(8):
                        empty(U[0:n].rearrange("p t (g c) -> p g t c", c=GC)[:, of_bank(q)],
                              lambda b: b[0:n, :].rearrange("p (g t c) -> p g t c", g=4, c=GC), ACT.Gelu_apprx_tanh)
                    for q in range(8):
                        empty(zT[:, :, 0:n, q], four(n))
                    i = 0
                    for h in range(NGL[t] // 4):
                        for f in range(4):
                            m = min(512, n * CH)
                            k = ngl(t) + 4 * h + f
                            if k >= 2:
                                act.wait_ge(so_ok, k - 1)
                            empty(gate[:, k % 2, 0:m], lambda b: b[:, 0:m], ACT.Sigmoid, bias=bglu[:, f:f + 1])

            @block.vector
            def _(dve):
                c = Count(dve, dve_own)
                tt = lambda o, a, b, op: c.step(dve.tensor_tensor(o, a, b, op))
                ts = lambda o, a, s1, s2, o1, o2: c.step(dve.tensor_scalar(o, a, s1, s2, o1, o2))
                dve.wait_ge(dt_ok, 1)
                dve.wait_ge(ld, 16 * NLD)
                c.up(dve.memset(MT[:], 0.0))
                c.wait()
                dve.tensor_tensor(S(X), lamr[:], S(DT), ALU.mult).then_inc(decay_in, 1)
                tt(S(TH), lami[:], S(DT), ALU.mult)
                for k, r, turn in ((K1, RS, 0.0), (K2, RC, 0.25)):
                    ts(S(k), S(TH), 1.0 / (2 * np.pi), turn, ALU.mult, ALU.add)
                    c.step(dve.tensor_scalar(S(k), S(k), ROUND, None, ALU.add))
                    c.step(dve.tensor_scalar(S(k), S(k), ROUND, None, ALU.subtract))
                    for part in (PI2_HI, PI2_LO):
                        c.step(dve.scalar_tensor_tensor(out=S(r), in0=S(k), scalar=-part, in1=S(TH if part == PI2_HI else r),
                                                        op0=ALU.mult, op1=ALU.add))
                    c.step(dve.tensor_scalar(S(r), S(r), turn * 2 * np.pi, None, ALU.add))
                    ins = dve.tensor_scalar(S(r), S(r), 3.1415925, -3.1415925, ALU.min, ALU.max)
                    if k == K2:
                        ins.then_inc(angles_ok, 1)
                    else:
                        c.step(ins)
                dve.wait_ge(decay_ok, 1)
                dve.wait_ge(trig_ok, 2)
                tt(S(AR), S(MAG), S(COS), ALU.mult)
                tt(S(AI), S(MAG), S(SIN), ALU.mult)
                tt(S(X), lamr[:], lamr[:], ALU.mult)
                tt(S(Y_), lami[:], lami[:], ALU.mult)
                tt(S(X), S(X), S(Y_), ALU.add)
                c.step(dve.reciprocal(S(DEN), S(X)))
                c.step(dve.tensor_scalar(S(W_), S(AR), -1.0, None, ALU.add))
                tt(S(X), S(W_), lamr[:], ALU.mult)
                tt(S(Y_), S(AI), lami[:], ALU.mult)
                tt(S(X), S(X), S(Y_), ALU.add)
                tt(S(CR), S(X), S(DEN), ALU.mult)
                tt(S(X), S(AI), lamr[:], ALU.mult)
                tt(S(Y_), S(W_), lami[:], ALU.mult)
                tt(S(X), S(X), S(Y_), ALU.subtract)
                tt(S(CI), S(X), S(DEN), ALU.mult)
                bc = lambda i: sm[:, i, :, None].to_broadcast([P, GP, GC])
                x16, y16 = wr[:, :, 0:GC], wi[:, :, 0:GC]
                complex_product(dve, c, BAr[:, :, CH - 1, :], BAi[:, :, CH - 1, :], br[:], bi[:], bc(CR), bc(CI), x16, y16)
                for j in range(CH - 2, -1, -1):
                    complex_product(dve, c, BAr[:, :, j, :], BAi[:, :, j, :], BAr[:, :, j + 1, :], BAi[:, :, j + 1, :],
                                    bc(AR), bc(AI), x16, y16)
                dve.tensor_scalar(S(W_), S(AI), -1.0, None, ALU.mult).then_inc(ba_ok, 1)
                dve.wait_ge(ba_ok, 1)
                c.step(dve.tensor_scalar(CAi[:, :, 0, :], CAi[:, :, 0, :], -1.0, None, ALU.mult))
                for l in range(1, CH + 1):
                    complex_product(dve, c, CAr[:, :, l, :], CAi[:, :, l, :], CAr[:, :, l - 1, :], CAi[:, :, l - 1, :],
                                    bc(AR), bc(W_), x16, y16)
                dve.memset(Hr[:, :, 0:1], 0.0).then_inc(ca_ok, 1)
                dve.memset(Hi[:, :, 0:1], 0.0).then_inc(h00_ok, 1)

                def unit(r, i):
                    tt(S(X), r, r, ALU.mult)
                    tt(S(Y_), i, i, ALU.mult)
                    tt(S(X), S(X), S(Y_), ALU.add)
                    ts(S(X), S(X), -0.5, 1.5, ALU.mult, ALU.add)
                    c.up(dve.tensor_tensor(r, r, S(X), ALU.mult))
                    tt(i, i, S(X), ALU.mult)

                for a, b in ((MAG, R8), (R8, R8), (R8, R8)):
                    tt(S(R8), S(a), S(a), ALU.mult)
                for n in range(3):
                    a_r, a_i = (COS, SIN) if n == 0 else (PR, PI_)
                    complex_product(dve, c, S(PR), S(PI_), S(a_r), S(a_i), S(a_r), S(a_i), S(K1), S(K2))
                    unit(S(PR), S(PI_))
                c.up(dve.tensor_copy(Tr[:, :, 0], S(PR)))
                c.step(dve.tensor_copy(Ti[:, :, 0], S(PI_)))
                m = 1
                while m < P:
                    if m > 1:
                        unit(Tr[:, :, m - 1], Ti[:, :, m - 1])
                    b_r, b_i = (z[:, :, m - 1:m].to_broadcast([P, GP, m]) for z in (Tr, Ti))
                    complex_product(dve, c, Tr[:, :, m:2 * m], Ti[:, :, m:2 * m], Tr[:, :, 0:m], Ti[:, :, 0:m], b_r, b_i,
                                    wr[:, :, 0:m], wi[:, :, 0:m])
                    m *= 2
                tt(S(AR), S(R8), S(PR), ALU.mult)
                tt(S(AI), S(R8), S(PI_), ALU.mult)
                dve.wait_ge(bank_free, 16)
                tt(eyed, ident[0:GC, None, 0:GC].to_broadcast([GC, G, GC]), dsk[:, :, None].to_broadcast([GC, G, GC]), ALU.mult)
                dve.tensor_tensor(KT[:, :, 0:GC], KT[:, :, 0:GC], eyed, ALU.add).then_inc(kt_ok, 1)
                dve.memset(gate[:, 0, 0:1], 0.0).then_inc(mt_zero, 1)
                dve.wait_ge(kt_ok, 1)
                dve.memset(gate[:, 1, 0:1], 0.0).then_inc(tab_ok, 1)
                for t, n in enumerate(CT):
                    dve.wait_ge(bank_free, base(t) + W)
                    a, b = dv[:, 0], dv[:, 1]
                    if t < 2:
                        tt(a, Tr[:], wr[:], ALU.mult)
                        tt(b, Ti[:], wi[:], ALU.mult)
                        tt(a, a, b, ALU.add)
                        dve.wait_ge(vi_ok, t + 1)
                        for g in range(GP):
                            r8 = sm[:, R8, g:g + 1].to_broadcast([P, P])
                            h_r = 0.0 if t == 0 else Hr[:, g, 0:1]
                            h_i = 0.0 if t == 0 else Hi[:, g, 0:1]
                            c.up(dve.tensor_tensor_scan(wr[:, g, :], r8, a[:, g, :], h_r, ALU.mult, ALU.add))
                            ins = dve.tensor_tensor_scan(wi[:, g, :], r8, pv[:, 0, g, :], h_i, ALU.mult, ALU.add)
                            if g < GP - 1:
                                c.up(ins)
                        ins.then_inc(scan_ok, 1)
                        dve.wait_ge(scan_ok, t + 1)
                        tt(a, Tr[:], wr[:], ALU.mult)
                        tt(b, Ti[:], wi[:], ALU.mult)
                        if t:
                            dve.wait_ge(bank_full, base(t - 1) + Y)
                        dve.tensor_tensor(Hr[:, :, 1:P + 1], a, b, ALU.subtract).then_inc(hr_ok, 1)
                        dve.wait_ge(hr_ok, t + 1)
                        dve.wait_ge(hi_ok, t + 1)
                        if t == 0:
                            dve.wait_ge(bank_full, base(t) + Y)
                            c.up(dve.tensor_copy(Hr[:, :, 0], Hr[:, :, P]))
                            c.wait()
                            dve.tensor_copy(Hi[:, :, 0], Hi[:, :, P]).then_inc(carry_ok, 1)
                            dve.wait_ge(carry_ok, 1)
                        else:
                            c.up(dve.tensor_copy(fin_p[:, 0], Hr[:, :, P]))
                            dve.tensor_copy(fin_p[:, 1], Hi[:, :, P]).then_inc(fin_ok, 1)
                    else:
                        b8 = lambda i: sm[:, i, :, None].to_broadcast([P, GP, DECB])
                        x, y = a[:, :, 0:DECB], b[:, :, 0:DECB]
                        for k, (p, q, op, w) in enumerate(((AR, AI, ALU.subtract, wr), (AI, AR, ALU.add, wi))):
                            c.up(dve.tensor_tensor(x, h0r[:, :, 0:DECB], b8(p), ALU.mult))
                            tt(y, h0i[:, :, 0:DECB], b8(q), ALU.mult)
                            tt(x, x, y, op)
                            tt(fin_s[:, k], x, w[:, :, 0:DECB], ALU.add)
                        dve.memset(dv[:, 0, 0, 0:1], 0.0).then_inc(fin_ok, 1)
                        dve.wait_ge(fin_ok, 2)
                    for h in range(NGL[t] // 4):
                        for f in range(4):
                            dve.wait_ge(bank_free, base(t) + ZT + 4 * h + f + 1)
                            k, m = ngl(t) + 4 * h + f, min(512, n * CH) // CH
                            dve.tensor_tensor(so[:, f, 64 * h:64 * h + m, :], zT[:, f, 64 * h:64 * h + m, :],
                                              gate[:, k % 2, 0:m * CH].rearrange("p (n t) -> p n t", t=CH), ALU.mult).then_inc(so_ok, 1)

            @block.gpsimd
            def _(pool):
                c = Count(pool, pool_own)
                for t, n in enumerate(CT):
                    pool.wait_ge(u_ld[t], 16)
                    if t == 0:
                        pool.wait_ge(bank_full, 16)
                    else:
                        pool.wait_ge(so_st, 64 * t)
                    pool.tensor_copy(Urv[0:n], U[0:n].rearrange("p j (g c) -> p g j c", c=GC)).then_inc(ur_ok, 1)
                    if t == 2:
                        break
                    pool.wait_ge(bank_free, base(t) + W)
                    a, b = pv[:, 0], pv[:, 1]
                    c.up(pool.tensor_tensor(a, Tr[:], wi[:], ALU.mult))
                    c.up(pool.tensor_tensor(b, Ti[:], wr[:], ALU.mult))
                    c.wait()
                    pool.tensor_tensor(a, a, b, ALU.subtract).then_inc(vi_ok, 1)
                    pool.wait_ge(scan_ok, t + 1)
                    c.up(pool.tensor_tensor(a, Tr[:], wi[:], ALU.mult))
                    c.up(pool.tensor_tensor(b, Ti[:], wr[:], ALU.mult))
                    c.wait()
                    if t:
                        pool.wait_ge(bank_full, base(t - 1) + Y)
                    pool.tensor_tensor(Hi[:, :, 1:P + 1], a, b, ALU.add).then_inc(hi_ok, 1)

            @block.tensor
            def _(pe):
                filled = [0]

                def bank():
                    i = filled[0]
                    filled[0] += 1
                    if i >= 8:
                        pe.wait_ge(bank_free, i - 7)
                    return ps[i % 8]

                pe.wait_ge(ba_ok, 1)
                for BA in (BAr, BAi):
                    for q in range(4):
                        b = bank()
                        for g in range(4):
                            mm = pe.transpose(b[:, g * P:(g + 1) * P], BA[:, 4 * q + g].rearrange("p j c -> p (j c)"), ident[:])
                        mm.then_inc(bank_full, 1)
                pe.wait_ge(ca_ok, 1)
                half = lambda g: slice((g % 2) * SS, (g % 2) * SS + SS)
                for q in range(8):
                    b = bank()
                    for i, g in enumerate(range(*of_bank(q).indices(G))):
                        for k, (BA, CA) in enumerate(((BAr, CAr), (BAi, CAi))):
                            mm = pe.matmul(b[0:GC, i * P:(i + 1) * P], BA[half(g), g // 2, CH - 1, :],
                                           CA[half(g), g // 2, 0:CH, :], start=k == 0, stop=k == 1)
                    mm.then_inc(bank_full, 1)
                for t, n in enumerate(CT):
                    pe.wait_ge(ur_ok, t + 1)
                    for q in range(8):
                        b = bank()
                        for g in range(4):
                            mm = pe.transpose(b[:, g * P:g * P + n], Urj[0:n, 4 * q + g, :], ident[0:n, 0:n])
                        mm.then_inc(bank_full, 1)
                    pe.wait_ge(bank_free, base(t) + U8)
                    for BT in (BTr, BTi):
                        for q in range(4):
                            b = bank()
                            for g in range(8 * q, 8 * q + 8):
                                k = (g // 2) % 4
                                mm = pe.matmul(b[half(g), k * P:k * P + n], BT[:, g // 2, half(g)], u8[:, g, 0:n],
                                               start=True, stop=True)
                            mm.then_inc(bank_full, 1)
                    if t == 0:
                        pe.wait_ge(mt_ok, 16 * CH)
                        pe.wait_ge(h00_ok, 1)
                    if t == 1:
                        pe.wait_ge(carry_ok, 1)
                    if t < 2:
                        pe.wait_ge(hr_ok, t + 1)
                        pe.wait_ge(hi_ok, t + 1)
                    h_r, h_i = (Hr, Hi) if t < 2 else (h0r, h0i)
                    for q in range(8):
                        b = bank()
                        for i, g in enumerate(range(*of_bank(q).indices(G))):
                            o = b[0:n, i * P:(i + 1) * P]
                            pe.matmul(o, u8[:, g, 0:n], MT[:, g, :], start=True, stop=False)
                            pe.matmul(o, h_r[half(g), g // 2, 0:n], CAr[half(g), g // 2, 1:CH + 1, :], start=False, stop=False)
                            mm = pe.matmul(o, h_i[half(g), g // 2, 0:n], CAi[half(g), g // 2, 1:CH + 1, :], start=False, stop=True)
                        mm.then_inc(bank_full, 1)
                    pe.wait_ge(bank_free, base(t) + Y)
                    for q in range(8):
                        b = bank()
                        for f in range(4):
                            mm = pe.transpose(b[:, f * P:f * P + n], U[0:n, q, f * P:(f + 1) * P], ident[0:n, 0:n])
                        mm.then_inc(bank_full, 1)
                    pe.wait_ge(bank_free, base(t) + ZT)
                    for h in range(NGL[t] // 4):
                        m = min(512, n * CH)
                        for f in range(4):
                            b = bank()
                            for k in range(4):
                                mm = pe.matmul(b[:, 0:m], wglu[:, k, f * P:(f + 1) * P],
                                               zT[:, k, 64 * h:64 * h + m // CH, :], start=k == 0, stop=k == 3)
                            mm.then_inc(bank_full, 1)




def attend(nc, A, R, ident):
    RING = 3
    width = lambda t: (t + 1) * P
    banks = lambda t: -(-width(t) // 512)
    halves = lambda t: -(-width(t) // 1024)
    first = 2
    ROUNDS = TOPK // 8
    indexed = lambda t: range(first, NPT).count(t + 2)
    KC = 512
    PPC = KC // PAGE
    NC = PAST // KC
    NK = PAST + DECT
    SAMPLE_TILE = 6
    sample_at = {(SAMPLE_TILE - 1, NH - 1): ("query", 0)}
    for c in range(NC + 1):
        sample_at[SAMPLE_TILE + c // 2, 4 * (c % 2) + 1] = ("scored", c)
        sample_at[SAMPLE_TILE + c // 2, 4 * (c % 2) + 2] = ("weighed", c)
    RING_USES = []
    for t in range(NPT):
        for h in range(NH):
            if indexed(t) and h % 2 == 0:
                RING_USES.append(("index", t + 2, h // 2, banks(t + 2)))
            if (t, h) in sample_at:
                kind, c = sample_at[t, h]
                RING_USES.append((kind, c, 0, 2 if kind == "scored" else 1))
            RING_USES.append(("attend", t, h, banks(t)))
        RING_USES.append(("out", t, 0, 1))
    after, n = {}, 0
    for kind, t, h, m in RING_USES:
        n += m
        after[kind, t, h] = n
    score_at = lambda t: NH * sum(halves(s) for s in range(t))
    head_at = lambda t: NH * t
    index_at = lambda t: NIH * (t - first)
    with ExitStack() as ctx:
        sb = lambda n, s, d=F32: ctx.enter_context(nc.sbuf_tensor(n + "_sb3", s, d))
        sem = lambda n: ctx.enter_context(nc.semaphore(n))
        pst = lambda n, s: ctx.enter_context(nc.psum_tensor(n, s, F32))
        q = sb("q", [P, 2, 4, P])
        qi = sb("qi_a", [P, 2, 2, P])
        relu = sb("relu", [P, 2, SEQ])
        mask = sb("mask", [P, 4, SEQ])
        prob = sb("prob", [P, 2, SEQ])
        pT = sb("pT", [P, 3, 4, P])
        best = sb("best", [P, 8])
        mx = sb("mx", [P, 2, 2])
        nmx = sb("nmx", [P, 2])
        rsum = sb("rsum", [P, 2, NH])
        rinv = sb("rinv", [P, NH])
        o = sb("o", [P, 2, NH, HD])
        aT = sb("aT", [P, 2, 4, P])
        pt = sb("pt_s", [1, DECB * NPAGE], I32)
        qid = sb("qid", [NS, NIH, 2, HD])
        qiS = sb("qiS", [P, DECB, NIH, DECT])
        wcol = sb("wcol", [P, 2])
        sel = sb("sel", [P, 2, NS])
        wsel = sb("wsel", [P, 2, NS])
        newmask = sb("newmask", [NS, DECT])
        kic = sb("kic", [P, 2, DECB, KC])
        rl = sb("rl", [P, 4, KC])
        best_s = sb("best_s", [NS, 8])
        mask_s = R["mask_s"]
        s_ld, pt_ld, kic_ld = sem("s_ld"), sem("pt_ld"), [sem("kic_ld0"), sem("kic_ld1")]
        dup_ok, wsel_ok = sem("dup_ok"), sem("wsel_ok")
        ring = [pst(f"ring{i}", [P, 512]) for i in range(RING)]
        sc = pst("sc", [P, 2, 1024])
        po = pst("po", [P, NH, HD])
        q_ld, qi_ld = [sem("q_ld0"), sem("q_ld1")], [sem("qi_ld0"), sem("qi_ld1")]
        ring_full, ring_free = sem("ring_full"), sem("ring_free")
        relu_ok, comb_ok, mask0, causal_ok, mask_ok = (sem(x) for x in ("relu_ok", "comb_ok", "mask0", "causal_ok", "mask_ok"))
        sc_full, sc_free, nmx_ok, prob_ok = (sem(x) for x in ("sc_full", "sc_free", "nmx_ok", "prob_ok"))
        pT_used, o_ok = sem("pT_used"), sem("o_ok")
        aT_st = [sem("aT_st0"), sem("aT_st1")]
        dve_own = sem("dve_own3")
        with nc.Block() as block:
            @block.sync
            def _(sp):
                def load_index(t):
                    if t >= first + 2:
                        sp.wait_ge(ring_full, after["index", t - 2, NIH - 1])
                    sp.dma_start(qi[:, t % 2], A["qi_d"][t]).then_inc(qi_ld[t % 2], 16)

                def load_query(t):
                    if t >= 2:
                        sp.wait_ge(sc_full, score_at(t - 1))
                    sp.dma_start(q[:, t % 2], A["q_d"][t]).then_inc(q_ld[t % 2], 16)

                def store(t):
                    sp.wait_ge(ring_free, after["out", t, 0])
                    sp.dma_start(A["a_d"][t], aT[:, t % 2]).then_inc(aT_st[t % 2], 16)

                def load_pages(c):
                    if c >= 2:
                        sp.wait_ge(ring_full, after["scored", 2 * c - 3, 0])
                    for b in range(DECB):
                        for half in range(2):
                            for p in range(PPC):
                                at = b * NPAGE + (c + half * NC // 2) * PPC + p
                                r = sp.value_load(pt[0:1, at:at + 1], min_val=0, max_val=A["kidxT_pages"].shape[0] - 1)
                                sp.dma_start(kic[HD * half:HD * half + HD, c % 2, b, p * PAGE:(p + 1) * PAGE],
                                             A["kidxT_pages"][bass.ds(r, 1)].rearrange("o d t -> (o d) t")).then_inc(kic_ld[c % 2], 16)

                load_query(0)
                load_index(first)
                sp.dma_start(pt[:], A["page_table"]).then_inc(pt_ld, 16)
                sp.dma_start(sel[:], A["sel"]).then_inc(s_ld, 16)
                sp.dma_start(newmask[:], A["newmask"]).then_inc(s_ld, 16)
                for b in range(DECB):
                    sp.dma_start(wcol[32 * (b % 4):32 * (b % 4) + 32, b // 4:b // 4 + 1],
                                 A["wi_d"][b * DECT:(b + 1) * DECT, :].rearrange("t (h o) -> h t o", o=1),
                                 allow_slow_non_contiguous=True).then_inc(s_ld, 16)
                sp.wait_ge(pt_ld, 16)
                for t in range(NPT):
                    if t + 1 < NPT:
                        load_query(t + 1)
                    if first <= t + 3 < NPT:
                        load_index(t + 3)
                    if t:
                        store(t - 1)
                    if t in (SAMPLE_TILE - 3, SAMPLE_TILE - 2):
                        load_pages(t - SAMPLE_TILE + 3)
                    if t in (SAMPLE_TILE + 1, SAMPLE_TILE + 2):
                        load_pages(t - SAMPLE_TILE + 1)
                store(NPT - 1)
                for i in range(2):
                    sp.wait_ge(aT_st[i], 16 * (NPT // 2))

            @block.tensor
            def _(pe):
                filled, scored = [0], [0]

                def bank():
                    i = filled[0]
                    filled[0] += 1
                    if i >= RING:
                        pe.wait_ge(ring_free, i - RING + 1)
                    return ring[i % RING]

                def index(t, h):
                    pe.wait_ge(qi_ld[t % 2], 16 * ((t - first) // 2 + 1))
                    rows = slice(HD * (h % 2), HD * (h % 2) + HD)
                    for b in range(banks(t)):
                        m = min(512, width(t) - 512 * b)
                        pe.matmul(bank()[:, 0:m], qi[rows, t % 2, h // 2, :], R["kiT"][rows, 512 * b:512 * b + m],
                                  start=True, stop=True).then_inc(ring_full, 1)

                def sample_part(kind, c):
                    half = c % 2
                    rows, m = slice(HD * half, HD * half + HD), KC if c < NC else DECT
                    if kind == "query":
                        pe.wait_ge(dup_ok, 2)
                        x = bank()
                        for h in range(NIH):
                            mm = pe.transpose(x[:, h * NS:(h + 1) * NS], qid[:, h].rearrange("p k d -> p (k d)"), ident[0:NS, 0:NS])
                        mm.then_inc(ring_full, 1)
                    elif kind == "scored":
                        pe.wait_ge(ring_free, after["query", 0, 0])
                        if c < NC:
                            pe.wait_ge(kic_ld[(c // 2) % 2], 16 * 2 * DECB * PPC * (c // 4 + 1))
                        for k in range(2):
                            x = bank()
                            for b in range(4 * k, 4 * k + 4):
                                src = kic[rows, (c // 2) % 2, b, :] if c < NC else R["kiT"][rows, SEQ + b * DECT:SEQ + (b + 1) * DECT]
                                mm = pe.matmul(x[32 * (b % 4):32 * (b % 4) + 32, 0:m], qiS[rows, b].rearrange("p h t -> p (h t)"), src,
                                               start=True, stop=True)
                            mm.then_inc(ring_full, 1)
                    else:
                        pe.wait_ge(wsel_ok, 2)
                        pe.wait_ge(ring_free, after["scored", c, 0])
                        x = bank()
                        for k in range(2):
                            mm = pe.matmul(x[0:NS, 0:m], wsel[:, k, :], rl[:, (2 * c + k) % 4, 0:m], start=k == 0, stop=k == 1)
                        mm.then_inc(ring_full, 1)

                def scores(t, h):
                    n, a = divmod(h, QPK)
                    rows = slice(HD * n, HD * n + HD)
                    for u in range(halves(t)):
                        i = scored[0]
                        scored[0] += 1
                        if i >= 2:
                            pe.wait_ge(sc_free, i - 1)
                        for b in range(2 * u, min(2 * u + 2, banks(t))):
                            m = min(512, width(t) - 512 * b)
                            mm = pe.matmul(sc[:, i % 2, 512 * (b - 2 * u):512 * (b - 2 * u) + m], q[rows, t % 2, a, :],
                                           R["kT"][rows, 512 * b:512 * b + m], start=True, stop=True)
                        mm.then_inc(sc_full, 1)

                def values(t, h, b, i):
                    pe.wait_ge(ring_free, i + 1)
                    if h == 0 and b == 0 and t:
                        pe.wait_ge(o_ok, t)
                    n = h // QPK
                    for k in range(4 * b, min(4 * b + 4, t + 1)):
                        mm = pe.matmul(po[:, h, :], pT[:, pt_of[i] % 3, k - 4 * b, :], R["V"][:, k, HD * n:HD * n + HD],
                                       start=k == 0, stop=k == t)
                    mm.then_inc(pT_used, 1)

                pt_of = {}

                def attend_tile(t):
                    pe.wait_ge(q_ld[t % 2], 16 * (t // 2 + 1))
                    scores(t, 0)
                    waiting = []
                    for h in range(NH):
                        if h + 1 < NH:
                            scores(t, h + 1)
                        if indexed(t) and h % 2 == 0:
                            index(t + 2, h // 2)
                        if (t, h) in sample_at:
                            sample_part(*sample_at[t, h])
                        pe.wait_ge(prob_ok, head_at(t) + h + 1)
                        for b in range(banks(t)):
                            i = filled[0]
                            x = bank()
                            pt_of[i] = len(pt_of)
                            for k in range(4 * b, min(4 * b + 4, t + 1)):
                                mm = pe.transpose(x[:, (k - 4 * b) * P:(k - 4 * b + 1) * P],
                                                  prob[:, h % 2, k * P:(k + 1) * P], ident[:])
                            mm.then_inc(ring_full, 1)
                            if waiting:
                                values(*waiting.pop())
                            waiting.append((t, h, b, i))
                    values(*waiting.pop())
                    pe.wait_ge(o_ok, t + 1)
                    x = bank()
                    for f in range(4):
                        mm = pe.transpose(x[:, f * P:(f + 1) * P], o[:, t % 2, 2 * f:2 * f + 2, :].rearrange("p h d -> p (h d)"), ident[:])
                    mm.then_inc(ring_full, 1)

                for t in range(NPT):
                    attend_tile(t)

            @block.scalar
            def _(act):
                emptied, turned_n = [0], [0]

                def empty(out, fn, func=ACT.Copy):
                    i = emptied[0]
                    emptied[0] += 1
                    act.wait_ge(ring_full, i + 1)
                    return act.activation(out, fn(ring[i % RING]), func).then_inc(ring_free, 1)

                def index(t, h):
                    k = index_at(t) + h
                    if k >= 2:
                        act.wait_ge(comb_ok, k - 1)
                    for b in range(banks(t)):
                        m = min(512, width(t) - 512 * b)
                        empty(relu[:, k % 2, 512 * b:512 * b + m], lambda x: x[:, 0:m], ACT.Relu)

                def sample_part(kind, c):
                    m = KC if c < NC else DECT
                    if kind == "query":
                        empty(qiS[:].rearrange("p b h t -> p h b t"),
                              lambda x: x[:, 0:NIH * NS].rearrange("p (h b t) -> p h b t", h=NIH, t=DECT))
                    elif kind == "scored":
                        for k in range(2):
                            if c >= 2:
                                act.wait_ge(ring_full, after["weighed", c - 2, 0])
                            empty(rl[:, (2 * c + k) % 4, 0:m], lambda x: x[:, 0:m], ACT.Relu)
                    else:
                        at = ((c % 2) * NC // 2 + c // 2) * KC if c < NC else PAST
                        empty(mask_s[:, at:at + m], lambda x: x[0:NS, 0:m])

                def attend_tile(t):
                    for h in range(NH):
                        if indexed(t) and h % 2 == 0:
                            index(t + 2, h // 2)
                        if (t, h) in sample_at:
                            sample_part(*sample_at[t, h])
                        act.wait_ge(nmx_ok, head_at(t) + h + 1)
                        act.activation(prob[:, h % 2, 0:width(t)], prob[:, h % 2, 0:width(t)], ACT.Exp, bias=nmx[:, h % 2:h % 2 + 1],
                                       scale=HD ** -0.5, accum_out=rsum[:, t % 2, h:h + 1]).then_inc(prob_ok, 1)
                        for b in range(banks(t)):
                            j = turned_n[0]
                            turned_n[0] += 1
                            if j >= 3:
                                act.wait_ge(pT_used, j - 2)
                            m = min(4, t + 1 - 4 * b)
                            empty(pT[:, j % 3, 0:m, :], lambda x: x[:, 0:m * P].rearrange("p (k q) -> p k q", q=P))
                    if t >= 2:
                        act.wait_ge(aT_st[t % 2], 16 * (t // 2))
                    i = emptied[0]
                    emptied[0] += 1
                    act.wait_ge(ring_full, i + 1)
                    act.activation(aT[:, t % 2], ring[i % RING][:].rearrange("p (f q) -> p f q", q=P), ACT.Copy).then_inc(ring_free, 1)

                for t in range(NPT):
                    attend_tile(t)

            @block.gpsimd
            def _(pool):
                pool.memset(mask[:, 0:2, :], 0.0).then_inc(mask0, 1)
                pool.wait_ge(mask0, 1)
                for t in range(2):
                    d = mask[:, t, t * P:(t + 1) * P]
                    pool.affine_select(out=d, in_=d, compare_op=ALU.is_ge, fill=NEG, base=0, pattern=[[-1, P]],
                                       channel_multiplier=1).then_inc(causal_ok, 1)
                for k in range(2):
                    pool.tensor_copy(qid[:, :, k, :], R["qi_s"][:, 0:NIH, :]).then_inc(dup_ok, 1)
                for t in range(first, NPT):
                    pool.wait_ge(comb_ok, index_at(t) + NIH)
                    d = mask[:, t % 4, t * P:(t + 1) * P]
                    pool.affine_select(out=d, in_=d, compare_op=ALU.is_ge, fill=NEG, base=0, pattern=[[-1, P]],
                                       channel_multiplier=1).then_inc(causal_ok, 1)

            @block.vector
            def _(dve):
                c = Count(dve, dve_own)
                scored = [0]

                def combine(t, h):
                    s = mask[:, t % 4, 0:width(t)]
                    k = index_at(t) + h
                    dve.wait_ge(ring_free, after["index", t, h])
                    r, w = relu[:, k % 2, 0:width(t)], R["wi"][:, t, h:h + 1]
                    if h == 0:
                        dve.tensor_scalar(s, r, w, None, ALU.mult).then_inc(comb_ok, 1)
                    else:
                        dve.wait_ge(comb_ok, k)
                        dve.scalar_tensor_tensor(out=s, in0=r, scalar=w, in1=s, op0=ALU.mult, op1=ALU.add).then_inc(comb_ok, 1)

                def choose(t, rounds):
                    s = mask[:, t % 4, 0:width(t)]
                    dve.wait_ge(causal_ok, t + 1)
                    for r in rounds:
                        c.step(dve.max(best[:], s))
                        c.step(dve.match_replace(s, best[:], s, TAKEN))
                    if ROUNDS - 1 in rounds:
                        dve.tensor_scalar(s, s, TAKEN, NEG, ALU.is_gt, ALU.mult).then_inc(mask_ok, 1)
                        dve.wait_ge(mask_ok, t - first + 1)

                def choose_samples(rounds):
                    if 0 in rounds:
                        dve.wait_ge(ring_free, after["weighed", NC, 0])
                        c.step(dve.tensor_tensor(mask_s[:, PAST:NK], mask_s[:, PAST:NK], newmask[:], ALU.add))
                    for r in rounds:
                        c.step(dve.max(best_s[:], mask_s[:]))
                        c.step(dve.match_replace(mask_s[:], best_s[:], mask_s[:], TAKEN))
                    if ROUNDS - 1 in rounds:
                        c.step(dve.tensor_scalar(mask_s[:], mask_s[:], TAKEN, NEG, ALU.is_gt, ALU.mult))

                def attend_tile(t):
                    for h in range(NH):
                        for u in range(halves(t)):
                            i = scored[0]
                            scored[0] += 1
                            m = min(1024, width(t) - 1024 * u)
                            dve.wait_ge(sc_full, i + 1)
                            if u == 0 and head_at(t) + h >= 2:
                                dve.wait_ge(ring_full, after["attend", t, h - 2] if h >= 2 else after["attend", t - 1, h + NH - 2])
                            init = -3e38 if u == 0 else mx[:, h % 2, u - 1:u]
                            dve.tensor_tensor_reduce(out=prob[:, h % 2, 1024 * u:1024 * u + m], in0=sc[:, i % 2, 0:m],
                                                          in1=mask[:, t % 4, 1024 * u:1024 * u + m], scale=1.0, scalar=init,
                                                          op0=ALU.add, op1=ALU.max, accum_out=mx[:, h % 2, u:u + 1]).then_inc(sc_free, 1)
                            dve.wait_ge(sc_free, i + 1)
                        dve.tensor_scalar(nmx[:, h % 2:h % 2 + 1], mx[:, h % 2, u:u + 1], -HD ** -0.5, None,
                                          ALU.mult).then_inc(nmx_ok, 1)
                        if first <= t + 1 < NPT:
                            choose(t + 1, range(ROUNDS // NH * h, ROUNDS // NH * (h + 1)))
                        if t == NPT - 1:
                            choose_samples(range(ROUNDS // NH * h, ROUNDS // NH * (h + 1)))
                        if indexed(t) and h % 2 == 0:
                            combine(t + 2, h // 2)
                    dve.wait_ge(prob_ok, head_at(t) + NH)
                    c.step(dve.reciprocal(rinv[:], rsum[:, t % 2, :]))
                    dve.wait_ge(pT_used, NH * sum(banks(s) for s in range(t + 1)))
                    if t >= 2:
                        dve.wait_ge(ring_full, after["out", t - 2, 0])
                    dve.tensor_tensor(o[:, t % 2], po[:], rinv[:, :, None].to_broadcast([P, NH, HD]), ALU.mult).then_inc(o_ok, 1)

                dve.wait_ge(s_ld, 16 * (2 + DECB))
                for k in range(2):
                    dve.tensor_scalar(wsel[:, k, :], sel[:, k, :], wcol[:, k:k + 1], None, ALU.mult).then_inc(wsel_ok, 1)
                dve.wait_ge(causal_ok, 2)
                for t in range(NPT):
                    attend_tile(t)




def attend_samples(nc, A, R, ident):
    RING = 6
    KC = 512
    PPC = KC // PAGE
    NC = PAST // KC
    NK = PAST + DECT
    NPAIR = DECB // 2
    SLOTS = 13
    PER = (NC + 1) + (NC + 1) + 1
    with ExitStack() as ctx:
        sb = lambda n, s, d=F32: ctx.enter_context(nc.sbuf_tensor(n + "_sb4", s, d))
        sem = lambda n: ctx.enter_context(nc.semaphore(n))
        pst = lambda n, s: ctx.enter_context(nc.psum_tensor(n, s, F32))
        pt = sb("pt_s", [1, DECB * NPAGE], I32)
        q16 = sb("q16", [P, 4, P])
        qz = sb("qz", [P, DECB, NKV, QPK, DECT])
        rep = sb("rep", [NS, DECB, NS])
        mask = R["mask_s"]
        kv = sb("kv", [P, SLOTS, 2, PPC, 2, P])
        vn = sb("vn", [DECT, DECB, P])
        prob = sb("prob_s", [P, NK])
        mx, nmx, rsum, rinv = (sb(n, [P, 1]) for n in ("mx_s", "nmx_s", "rsum_s", "rinv_s"))
        pT = sb("pT_s", [P, 3, 4, P])
        o2 = sb("o2", [P, 2, HD])
        aT = sb("aT_s", [P, 4, P])
        ring = [pst(f"rs{i}", [P, KC]) for i in range(RING)]
        po = pst("po_s", [P, P])
        ld, pt_ld, q_ld = sem("ld4"), sem("pt_ld4"), sem("q_ld4")
        kv_ld = [sem(f"kv_ld{i}_") for i in range(SLOTS)]
        ring_full, ring_free, prep = sem("ring_full4"), sem("ring_free4"), sem("prep")
        own, nmx_ok, prob_ok, pT_used, o_ok, st = (sem(x) for x in ("own4", "nmx_ok4", "prob_ok4", "pT_used4", "o_ok4", "st4"))
        sc_ok = sem("sc_ok")
        with nc.Block() as block:
            @block.sync
            def _(sp):
                sp.dma_start(pt[:], A["page_table"]).then_inc(pt_ld, 16)
                sp.dma_start(q16[:], A["q_d"][NPT]).then_inc(q_ld, 16)
                sp.dma_start(rep[:], A["rep"]).then_inc(ld, 16)
                sp.dma_start(vn[:], A["v_s"].rearrange("(b t) c -> t b c", t=DECT)).then_inc(ld, 16)
                sp.wait_ge(pt_ld, 16)
                for i in range(NPAIR * NC):
                    pair, c = divmod(i, NC)
                    if i >= SLOTS:
                        q, d = divmod(i - SLOTS, NC)
                        sp.wait_ge(pT_used, (NC + 1) * q + d + 1)
                    for b in range(2):
                        for p in range(PPC):
                            at = (2 * pair + b) * NPAGE + c * PPC + p
                            r = sp.value_load(pt[0:1, at:at + 1], min_val=0, max_val=A["kv_pages"].shape[0] - 1)
                            sp.dma_start(kv[:, i % SLOTS, b, p], A["kv_pages"][bass.ds(r, 1)].rearrange("o p k c -> (o p) k c")
                                         ).then_inc(kv_ld[i % SLOTS], 16)
                sp.wait_ge(ring_free, PER * NPAIR)
                sp.dma_start(A["a_d"][NPT], aT[:]).then_inc(st, 16)
                sp.wait_ge(st, 16)

            @block.gpsimd
            def _(pool):
                pool.memset(qz[:], 0.0).then_inc(prep, 1)
                pool.memset(aT[:], 0.0).then_inc(prep, 1)
                pool.wait_ge(q_ld, 16)
                pool.wait_ge(prep, 2)
                for n in range(NKV):
                    rows = slice(HD * n, HD * n + HD)
                    pool.tensor_copy(qz[rows, :, n], q16[rows, :, 0:NS].rearrange("p a (b t) -> p b a t", t=DECT)).then_inc(prep, 1)

            @block.vector
            def _(dve):
                c = Count(dve, own)
                for pair in range(NPAIR):
                    dve.wait_ge(ring_free, PER * pair + NC + 1)
                    c.step(dve.tensor_reduce(mx[:], prob[:], AX.X, ALU.max))
                    dve.tensor_scalar(nmx[:], mx[:], -HD ** -0.5, None, ALU.mult).then_inc(nmx_ok, 1)
                    dve.wait_ge(prob_ok, pair + 1)
                    c.step(dve.reciprocal(rinv[:], rsum[:]))
                    dve.wait_ge(pT_used, (NC + 1) * (pair + 1))
                    if pair:
                        dve.wait_ge(ring_full, PER * pair)
                    for r in range(4):
                        rows, n = slice(32 * r, 32 * r + 32), r % 2
                        for k in range(2):
                            dve.tensor_scalar(o2[rows, k, :], po[rows, HD * n:HD * n + HD], rinv[rows, :], None, ALU.mult).then_inc(o_ok, 1)

            @block.scalar
            def _(act):
                emptied = [0]

                def empty(out, fn, func=ACT.Copy):
                    i = emptied[0]
                    emptied[0] += 1
                    act.wait_ge(ring_full, i + 1)
                    act.activation(out, fn(ring[i % RING]), func).then_inc(ring_free, 1)

                for pair in range(NPAIR):
                    for c in range(NC + 1):
                        m = KC if c < NC else DECT
                        empty(prob[:, c * KC:c * KC + m], lambda x: x[:, 0:m])
                    act.wait_ge(nmx_ok, pair + 1)
                    act.activation(prob[:], prob[:], ACT.Exp, bias=nmx[:], scale=HD ** -0.5, accum_out=rsum[:]).then_inc(prob_ok, 1)
                    for c in range(NC + 1):
                        j = (NC + 1) * pair + c
                        if j >= 3:
                            act.wait_ge(pT_used, j - 2)
                        if c < NC:
                            empty(pT[:, j % 3], lambda x: x[:].rearrange("p (k r) -> p k r", r=P))
                        else:
                            empty(pT[0:DECT, j % 3, 0, :], lambda x: x[0:DECT, 0:P])
                    i = emptied[0]
                    emptied[0] += 1
                    act.wait_ge(ring_full, i + 1)
                    if pair == 0:
                        act.wait_ge(prep, 2)
                    for par in range(2):
                        for b in range(2):
                            rows, tok = slice(HD * par, HD * par + HD), (2 * pair + b) * DECT
                            src = ring[i % RING][rows, b * 64:b * 64 + 64].rearrange("p (f a t) -> p f a t", a=2, t=DECT)[:, :, par, :]
                            ins = act.activation(aT[rows, :, tok:tok + DECT], src, ACT.Copy)
                            ins.then_inc(ring_free if par == b == 1 else sc_ok, 1)
                    act.wait_ge(sc_ok, 3 * (pair + 1))

            @block.tensor
            def _(pe):
                filled, turned = [0], [0]

                def bank():
                    i = filled[0]
                    filled[0] += 1
                    if i >= RING:
                        pe.wait_ge(ring_free, i - RING + 1)
                    return ring[i % RING]

                pe.wait_ge(prep, 4)
                pe.wait_ge(ld, 32)
                for pair in range(NPAIR):
                    for c in range(NC + 1):
                        m, i = (KC, pair * NC + c) if c < NC else (DECT, 0)
                        if c < NC:
                            pe.wait_ge(kv_ld[i % SLOTS], 16 * 2 * PPC * (i // SLOTS + 1))
                        x = bank()
                        for b in range(2):
                            s = 2 * pair + b
                            o = x[64 * b:64 * b + 64, 0:m]
                            k = kv[:, i % SLOTS, b, :, 0, :] if c < NC else R["kT"][:, SEQ + s * DECT:SEQ + (s + 1) * DECT]
                            pe.matmul(o, qz[:, s].rearrange("p n a t -> p (n a t)"), k, start=True, stop=False)
                            mm = pe.matmul(o, rep[:, s, :], mask[:, c * KC:c * KC + m], start=False, stop=True)
                        mm.then_inc(ring_full, 1)
                    pe.wait_ge(prob_ok, pair + 1)
                    if pair:
                        pe.wait_ge(o_ok, 8 * pair)
                    todo = []
                    for c in range(NC + 2):
                        if c <= NC:
                            i = filled[0]
                            x = bank()
                            for k in range(PPC if c < NC else 1):
                                at = c * KC + k * P
                                m = P if c < NC else DECT
                                mm = pe.transpose(x[0:m, k * P:(k + 1) * P], prob[:, at:at + m], ident[:])
                            mm.then_inc(ring_full, 1)
                            todo.append((c, i))
                        if c >= 1:
                            d, i = todo.pop(0)
                            pe.wait_ge(ring_free, i + 1)
                            j = turned[0]
                            turned[0] += 1
                            v = pair * NC + d
                            for b in range(2):
                                for k in range(PPC if d < NC else 1):
                                    if d < NC:
                                        l, r = pT[:, j % 3, k, 64 * b:64 * b + 64], kv[:, v % SLOTS, b, k, 1, :]
                                    else:
                                        l, r = pT[0:DECT, j % 3, 0, 64 * b:64 * b + 64], vn[:, 2 * pair + b, :]
                                    mm = pe.matmul(po[64 * b:64 * b + 64, :], l, r, start=d == 0 and k == 0, stop=d == NC)
                            mm.then_inc(pT_used, 1)
                    pe.wait_ge(o_ok, 8 * (pair + 1))
                    x = bank()
                    pe.transpose(x[:, 0:P], o2[:].rearrange("p k d -> p (k d)"), ident[:]).then_inc(ring_full, 1)




def mix_and_feed_forward(nc, A, R, ident):
    NG, TPG, KQ = 4, 4, 4
    MT_ = TPG + 1
    NSTEP = DFF // P // KQ
    RAW, RING = 4, 6
    tiles = lambda g: TPG + (g == NG - 1)
    nb = lambda g: 1 + (g == NG - 1)
    SPG = 8 + 4 + 8 * (NSTEP - 1) + 4
    STEP = (("u", 2), ("d", 0), ("u", 3), ("d", 1), ("d", 2), ("u", 0), ("d", 3), ("u", 1))
    STEP0 = (("u", 2), ("u", 0), ("u", 3), ("u", 1))
    LAST = STEP[:5] + STEP[6:7]

    def at(g, m, pos):
        off = {-1: 0, 0: 8}.get(m, 12) if isinstance(m, int) else 12
        k = 2 + off + pos
        turns = SPG // RAW * g + (2 * (m - 1) if not isinstance(m, int) or m >= 1 else 0)
        return k % RAW, turns + k // RAW

    def up_at(g, m, c):
        if isinstance(m, int) and m == 0:
            if c < 2:
                return (c, 0) if g == 0 else at(g - 1, NSTEP - 1, (5, 7)[c])
            return at(g, 0, (0, 2)[c - 2])
        if c >= 2:
            return at(g, m, (0, 2)[c - 2])
        if isinstance(m, int) and m == 1:
            return at(g, 0, (1, 3)[c])
        s, f = at(g, m, (5, 7)[c])
        return s, f - 2

    def down_at(g, k, c):
        if isinstance(k, int) and k < 0:
            return at(g, -1, 4 * (k + 2) + c)
        if isinstance(k, int) and k == NSTEP - 1:
            return at(g, NSTEP - 1, (6 if g == NG - 1 else 8) + c)
        if isinstance(k, int) and k == NSTEP - 2 and g == NG - 1:
            return at(g, NSTEP - 1, (1, 3, 4, 5)[c])
        return at(g, k + 1, (1, 3, 4, 6)[c])

    ring_group = lambda g: 4 * tiles(g) + NSTEP * (KQ * nb(g) + 2 * tiles(g))
    ring0 = lambda g: sum(ring_group(k) for k in range(g))
    first = lambda m: isinstance(m, int) and m == 0
    ring_up = lambda g, m: ring0(g) + 4 * tiles(g) + (KQ * nb(g) + 2 * tiles(g)) * m - (0 if first(m) else 2 * tiles(g))
    ring_down = lambda g, k: ring0(g) + ring_group(g) if isinstance(k, int) and k == NSTEP - 1 else ring_up(g, k + 1) + KQ * nb(g) + 2 * tiles(g)
    hid0 = lambda g: NSTEP * KQ * g
    sums0 = lambda g: sum(2 * tiles(k) * (NSTEP + 1) for k in range(g))
    tile0 = lambda g: TPG * g

    def norms(g):
        out = []
        for i in range(tiles(g) + 1):
            out += ([("mix", i)] if i < tiles(g) else []) + ([("pre", i - 1)] if i else [])
        return out + [("out", i) for i in range(tiles(g))]

    with ExitStack() as ctx:
        sb = lambda n, s, d=F32: ctx.enter_context(nc.sbuf_tensor(n + "_sb5", s, d))
        sem = lambda n: ctx.enter_context(nc.semaphore(n + "5"))
        pst = lambda n, s: ctx.enter_context(nc.psum_tensor(n, s, F32))
        raw = sb("raw", [P, RAW, D])
        up_hi, up_lo = sb("up_hi", [P, 2, D], F32R), sb("up_lo", [P, 2, D], F32R)
        dn_hi, dn_lo = sb("dn_hi", [P, KQ, D], F32R), sb("dn_lo", [P, KQ, D], F32R)
        x_hi, x_lo = sb("x_hi", [P, KD, MT_ * P], F32R), sb("x_lo", [P, KD, MT_ * P], F32R)
        h_hi, h_lo = sb("h_hi", [P, 2, KQ, MT_ * P], F32R), sb("h_lo", [P, 2, KQ, MT_ * P], F32R)
        hr = sb("hr", [P, 2, 512])
        feat = sb("feat", [P, 2, KQ, P])
        part = sb("part", [P, 2, 512])
        mix = sb("mix", [P, MT_, D])
        acc = sb("acc", [P, MT_, D])
        g_post, g_ffn = sb("g_post", [P, D]), sb("g_ffn", [P, D])
        g_pre = sb("g_pre", [P, KD])
        ssum, mean, root, rs = (sb(n, [P, 3 * NT]) for n in ("ssum", "mean", "root", "rs"))
        newton = sb("newton", [P, 1])
        ring = [pst(f"r5_{i}", [P, 512]) for i in range(RING)]
        tp = [pst(f"tp{i}", [P, 4, P]) for i in range(2)]
        ld, raw_ld, raw_used = sem("ld"), [sem(f"raw_ld{i}_") for i in range(RAW)], [sem(f"raw_used{i}_") for i in range(RAW)]
        feat_ld, x_ld = [sem("feat_ld0_"), sem("feat_ld1_")], sem("x_ld")
        w_hi_ok = [sem(f"w_hi_ok{i}_") for i in range(RAW)]
        ring_full, ring_free = sem("ring_full"), sem("ring_free")
        f_hi_ok, f_lo_ok, sq_ok, h_hi_ok, h_lo_ok = (sem(x) for x in ("f_hi_ok", "f_lo_ok", "sq_ok", "h_hi_ok", "h_lo_ok"))
        sum_ok, zero_ok = sem("sum_ok"), sem("zero_ok")
        ss_ok, mean_ok, root_ok, rs_ok, newt = (sem(x) for x in ("ss_ok", "mean_ok", "root_ok", "rs_ok", "newt"))
        res_ok, xn_ok, tp_full, x_hi_ok, x_lo_ok, own, y_ok, y_st = (sem(x) for x in ("res_ok", "xn_ok", "tp_full", "x_hi_ok", "x_lo_ok", "own", "y_ok", "y_st"))

        def wait(eng, s, value):
            if not (isinstance(value, int) and value <= 0):
                eng.wait_ge(s, value)

        def steps(eng, g, body):
            body(g, 0, 0)
            with eng.Fori(0, (NSTEP - 2) // 2) as i:
                for k in range(2):
                    body(g, 2 * i + 1 + k, 1 + k)
            body(g, NSTEP - 1, NSTEP - 1)

        def stream(g, m):
            if first(m):
                return [("u", 0 if c >= 2 else 1, c, at(g, 0, j)) for j, (_, c) in enumerate(STEP0)]
            last = isinstance(m, int) and m == NSTEP - 1
            return [(kind, (m if c >= 2 else m + 1) if kind == "u" else m - 1, c, at(g, m, j))
                    for j, (kind, c) in enumerate(LAST if last and g == NG - 1 else STEP)]

        def by_chunk(g, m, c):
            todo = stream(g, m)
            per = -(-len(todo) // KQ)
            return todo[per * c:per * c + per]

        with nc.Block() as block:
            @block.sync
            def _(sp):
                sp.dma_start(g_post[:], A["g_post"]).then_inc(ld, 16)
                sp.dma_start(g_ffn[:], A["g_ffn"]).then_inc(ld, 16)
                sp.dma_start(g_pre[:], A["g_ffn_pre"]).then_inc(ld, 16)

                def load(kind, m, c, where):
                    s, f = where
                    wait(sp, raw_used[s], f)
                    if isinstance(m, int) and m == NSTEP:
                        m = 0
                    src = A[{"o": "w_out", "u": "w_up", "d": "w_down"}[kind]][bass.ds(KQ * m + c, 1)]
                    sp.dma_start(raw[:, s, :], src.rearrange("o p n -> (o p) n")).then_inc(raw_ld[s], 16)

                def step(g, m, m0):
                    for kind, n, c, where in stream(g, m):
                        load(kind, n, c, where)

                for c in range(2):
                    load("u", 0, c, (c, 0))
                for g in range(NG):
                    for k in range(2):
                        for c in range(KQ):
                            load("o", k, c, down_at(g, k - 2, c))
                    steps(sp, g, step)
                    for c in range(KQ):
                        load("d", NSTEP - 1, c, down_at(g, NSTEP - 1, c))

            @block.gpsimd
            def _(pool):
                def sums(g, into, ring_at, done):
                    wait(pool, sum_ok, done)
                    for j in range(2 * tiles(g)):
                        pool.wait_ge(ring_free, ring_at + j + 1)
                        o = into[:, j // 2, 512 * (j % 2):512 * (j % 2) + 512]
                        pool.tensor_tensor(o, o, part[:, j % 2, :], ALU.add).then_inc(sum_ok, 1)

                def step(g, m, m0):
                    for c in range(KQ):
                        for b in range(nb(g)):
                            n = hid0(g) + (KQ * m + c) * nb(g) + b
                            w = 512 if b == 0 else NS
                            o = slice(512 * b, 512 * b + w)
                            pool.wait_ge(h_hi_ok, n + 1)
                            pool.tensor_tensor(h_lo[:, m0 % 2, c, o], hr[:, (c * nb(g) + b) % 2, 0:w],
                                               h_hi[:, m0 % 2, c, o].bitcast(F32), ALU.subtract).then_inc(h_lo_ok, 1)
                    if not first(m):
                        sums(g, acc, ring_up(g, m) + KQ * nb(g), sums0(g) + 2 * tiles(g) * m)

                for g in range(NG):
                    sums(g, mix, ring0(g) + 2 * tiles(g), sums0(g))
                    for i in range(tiles(g)):
                        pool.wait_ge(tp_full, 2 * (tile0(g) + i + 1))
                        pool.memset(acc[:, i, :], 0.0).then_inc(zero_ok, 1)
                    pool.wait_ge(zero_ok, tile0(g) + tiles(g))
                    steps(pool, g, step)
                    sums(g, acc, ring_down(g, NSTEP - 1) - 2 * tiles(g), sums0(g) + 2 * tiles(g) * NSTEP)

            def store(act, t):
                act.wait_ge(y_ok, t + 1)
                i = t % TPG if t < NPT else TPG
                if t < NPT:
                    act.dma_start(A["y_p"][t * P:(t + 1) * P, :], acc[:, i, :]).then_inc(y_st, 16)
                else:
                    act.dma_start(A["y_s"], acc[0:NS, i, :]).then_inc(y_st, 16)

            @block.scalar
            def _(act):
                def high(kind, g, n, c, where):
                    s, f = where
                    act.wait_ge(raw_ld[s], 16 * f + 16)
                    if kind == "u":
                        if c >= 2:
                            r = ring_up(g, n) + nb(g) * (c - 1)
                        elif isinstance(n, int) and n == NSTEP:
                            r = ring_up(g, n - 1) + nb(g) * (c + 3)
                        elif isinstance(n, int) and n == 1:
                            r = ring_up(g, 0) + nb(g) * (c + 3)
                        else:
                            r = ring_up(g, n) - 2 * tiles(g) - nb(g) * (1 - c)
                        act.wait_ge(ring_full, r)
                        hi = up_hi[:, c % 2]
                    else:
                        if isinstance(n, int) and n < 0:
                            r = ring0(g) + 2 * tiles(g) * (n + 2)
                        else:
                            r = ring0(g) + 4 * tiles(g) if isinstance(n, int) and n == 0 else ring_up(g, n) + KQ * nb(g) + 2 * tiles(g)
                        wait(act, ring_full, r)
                        hi = dn_hi[:, c]
                    act.activation(hi, raw[:, s, :], ACT.Copy).then_inc(w_hi_ok[s], 1)

                def sums(g, ring_at, at0, done, into=None):
                    for j in range(2 * tiles(g)):
                        act.wait_ge(ring_full, ring_at + j + 1)
                        if into is None:
                            o = part[:, j % 2, :]
                            wait(act, sum_ok, done + j - 1)
                        else:
                            o = into[:, j // 2, 512 * (j % 2):512 * (j % 2) + 512]
                        act.activation(o, ring[(at0 + j) % RING][:], ACT.Copy).then_inc(ring_free, 1)

                def square_sum(n, x):
                    act.activation(hr[:].rearrange("p a b -> p (a b)"), x, ACT.Square, accum_out=ssum[:, n:n + 1]).then_inc(ss_ok, 1)
                    act.wait_ge(mean_ok, n + 1)
                    act.activation(root[:, n:n + 1], mean[:, n:n + 1], ACT.Sqrt).then_inc(root_ok, 1)

                def step(g, m, m0):
                    for c in range(KQ):
                        for b in range(nb(g)):
                            n = hid0(g) + (KQ * m + c) * nb(g) + b
                            w = 512 if b == 0 else NS
                            k = c * nb(g) + b
                            act.wait_ge(ring_full, ring_up(g, m) + k + 1)
                            wait(act, h_lo_ok, n - 1)
                            s = hr[:, k % 2, 0:w]
                            act.activation(s, ring[(ring_up(g, m0) + k) % RING][:, 0:w], ACT.Relu).then_inc(ring_free, 1)
                            act.wait_ge(ring_free, ring_up(g, m) + k + 1)
                            act.activation(s, s, ACT.Square).then_inc(sq_ok, 1)
                            act.wait_ge(sq_ok, n + 1)
                            act.activation(h_hi[:, m0 % 2, c, 512 * b:512 * b + w], s, ACT.Copy).then_inc(h_hi_ok, 1)
                        for kind, nn, cc, where in by_chunk(g, m, c):
                            high(kind, g, nn, cc, where)
                    if not first(m):
                        sums(g, ring_up(g, m) + KQ * nb(g), ring_up(g, m0) + KQ * nb(g), sums0(g) + 2 * tiles(g) * m)

                def feature_load(g, n):
                    k, i = divmod(n, tiles(g))
                    at = 2 * tile0(g) + n
                    wait(act, f_lo_ok, at - 1)
                    act.dma_start(feat[:, at % 2], A["a_d" if k == 0 else "so_d"][tile0(g) + i]).then_inc(feat_ld[at % 2], 16)

                for c in range(2):
                    act.wait_ge(raw_ld[c], 16)
                    act.activation(up_hi[:, c], raw[:, c, :], ACT.Copy).then_inc(w_hi_ok[c], 1)
                act.wait_ge(ld, 48)
                for g in range(NG):
                    T = tiles(g)
                    wait(act, y_st, 16 * tile0(g))
                    for i in range(T):
                        act.dma_start(acc[:, i, :], A["x_all"][(tile0(g) + i) * P:(tile0(g) + i + 1) * P, :]).then_inc(x_ld, 16)
                    for n in range(2):
                        feature_load(g, n)
                    for c in range(KQ):
                        high("d", g, -2, c, down_at(g, -2, c))
                    wait(act, ring_full, ring0(g))
                    for n in range(2 * T):
                        k, i = divmod(n, T)
                        at_ = 2 * tile0(g) + n
                        act.wait_ge(feat_ld[at_ % 2], 16 * (at_ // 2 + 1))
                        act.activation(h_hi[:, k, :, i * P:(i + 1) * P], feat[:, at_ % 2], ACT.Copy).then_inc(f_hi_ok, 1)
                        if n + 2 < 2 * T:
                            feature_load(g, n + 2)
                    wait(act, y_ok, tile0(g))
                    sums(g, ring0(g), ring0(g), 0, into=mix)
                    for c in range(KQ):
                        high("d", g, -1, c, down_at(g, -1, c))
                    sums(g, ring0(g) + 2 * T, ring0(g) + 2 * T, sums0(g))
                    wait(act, h_lo_ok, hid0(g))
                    for k, (what, i) in enumerate(norms(g)):
                        t, n = tile0(g) + i, 3 * tile0(g) + k
                        if what == "out":
                            if i == 0:
                                steps(act, g, step)
                                for c in range(KQ):
                                    high("d", g, NSTEP - 1, c, down_at(g, NSTEP - 1, c))
                                sums(g, ring_down(g, NSTEP - 1) - 2 * T, ring_down(g, NSTEP - 1) - 2 * T, sums0(g) + 2 * T * NSTEP)
                                act.wait_ge(h_lo_ok, hid0(g) + NSTEP * KQ * nb(g))
                            act.wait_ge(sum_ok, sums0(g) + 2 * T * NSTEP + 2 * i + 2)
                            square_sum(n, acc[:, i, :])
                            if i:
                                store(act, t - 1)
                        elif what == "mix":
                            act.wait_ge(sum_ok, sums0(g) + 2 * i + 2)
                            square_sum(n, mix[:, i, :])
                        else:
                            act.wait_ge(res_ok, t + 1)
                            square_sum(n, mix[:, i, :])
                            for k_ in range(KD):
                                act.wait_ge(tp_full, 2 * t + 1 + k_ // 4)
                                act.activation(x_hi[:, k_, i * P:(i + 1) * P], tp[k_ // 4][:, k_ % 4, :], ACT.Copy,
                                               scale=g_pre[:, k_:k_ + 1]).then_inc(x_hi_ok, 1)
                    store(act, tile0(g) + T - 1)
                act.wait_ge(y_st, 16 * NT)

            @block.vector
            def _(dve):
                c = Count(dve, own)

                def low(kind, c, where):
                    s, f = where
                    dve.wait_ge(w_hi_ok[s], f + 1)
                    hi, lo = (up_hi[:, c % 2], up_lo[:, c % 2]) if kind == "u" else (dn_hi[:, c], dn_lo[:, c])
                    dve.tensor_tensor(lo, raw[:, s, :], hi.bitcast(F32), ALU.subtract).then_inc(raw_used[s], 1)

                def step(g, m, m0):
                    for kind, _, cc, where in stream(g, m):
                        low(kind, cc, where)

                def inverse(n):
                    dve.wait_ge(ss_ok, n + 1)
                    dve.tensor_scalar(mean[:, n:n + 1], ssum[:, n:n + 1], 1.0 / D, EPS, ALU.mult, ALU.add).then_inc(mean_ok, 1)
                    dve.wait_ge(root_ok, n + 1)
                    if n:
                        dve.wait_ge(rs_ok, n)
                    inverse_root(dve, rs[:, n:n + 1], mean[:, n:n + 1], root[:, n:n + 1], newton[:], newt, 4 * n).then_inc(rs_ok, 1)
                    dve.wait_ge(rs_ok, n + 1)
                    return rs[:, n:n + 1]

                for cc in range(2):
                    low("u", cc, (cc, 0))
                dve.wait_ge(ld, 48)
                for g in range(NG):
                    T = tiles(g)
                    for cc in range(KQ):
                        low("d", cc, down_at(g, -2, cc))
                    for n in range(2 * T):
                        k, i = divmod(n, T)
                        at_ = 2 * tile0(g) + n
                        dve.wait_ge(f_hi_ok, at_ + 1)
                        dve.tensor_tensor(h_lo[:, k, :, i * P:(i + 1) * P], feat[:, at_ % 2],
                                          h_hi[:, k, :, i * P:(i + 1) * P].bitcast(F32), ALU.subtract).then_inc(f_lo_ok, 1)
                    for cc in range(KQ):
                        low("d", cc, down_at(g, -1, cc))
                    dve.wait_ge(x_ld, 16 * (tile0(g) + T))
                    for k, (what, i) in enumerate(norms(g)):
                        t, n = tile0(g) + i, 3 * tile0(g) + k
                        if what == "out" and i == 0:
                            steps(dve, g, step)
                            for cc in range(KQ):
                                low("d", cc, down_at(g, NSTEP - 1, cc))
                        r = inverse(n)
                        if what == "mix":
                            c.step(dve.scalar_tensor_tensor(out=mix[:, i, :], in0=mix[:, i, :], scalar=r, in1=g_post[:],
                                                            op0=ALU.mult, op1=ALU.mult))
                            dve.tensor_tensor(mix[:, i, :], mix[:, i, :], acc[:, i, :], ALU.add).then_inc(res_ok, 1)
                        elif what == "pre":
                            dve.tensor_scalar(acc[:, i, :], mix[:, i, :], r, None, ALU.mult).then_inc(xn_ok, 1)
                            for k_ in range(KD):
                                dve.wait_ge(x_hi_ok, KD * t + 4 * (k_ // 4 + 1))
                                dve.scalar_tensor_tensor(out=x_lo[:, k_, i * P:(i + 1) * P], in0=tp[k_ // 4][:, k_ % 4, :],
                                                         scalar=g_pre[:, k_:k_ + 1], in1=x_hi[:, k_, i * P:(i + 1) * P].bitcast(F32),
                                                         op0=ALU.mult, op1=ALU.subtract).then_inc(x_lo_ok, 1)
                        else:
                            c.step(dve.scalar_tensor_tensor(out=acc[:, i, :], in0=acc[:, i, :], scalar=r, in1=g_ffn[:],
                                                            op0=ALU.mult, op1=ALU.mult))
                            dve.tensor_tensor(acc[:, i, :], acc[:, i, :], mix[:, i, :], ALU.add).then_inc(y_ok, 1)

            @block.tensor
            def _(pe):
                def bank(at, at0):
                    wait(pe, ring_free, at - RING + 1)
                    return ring[at0 % RING]

                def down(g, k, ring_at, at0, slot):
                    for c in range(KQ):
                        s, f = down_at(g, k, c)
                        pe.wait_ge(raw_used[s], f + 1)
                    for t in range(tiles(g)):
                        if isinstance(k, int) and k < 0:
                            pe.wait_ge(f_lo_ok, 2 * tile0(g) + (k + 2) * tiles(g) + t + 1)
                        tok = slice(t * P, (t + 1) * P)
                        for half in range(2):
                            j = 2 * t + half
                            o = bank(ring_at + j, at0 + j)
                            col = slice(512 * half, 512 * half + 512)
                            n = 0
                            for c in range(KQ):
                                for x, w in ((h_hi, dn_hi), (h_hi, dn_lo), (h_lo, dn_hi)):
                                    mm = pe.matmul(o[:], x[:, slot, c, tok], w[:, c, col], start=n == 0, stop=n == 3 * KQ - 1)
                                    n += 1
                            mm.then_inc(ring_full, 1)

                def step(g, m, m0):
                    for c in range(KQ):
                        s, f = up_at(g, m, c)
                        pe.wait_ge(raw_used[s], f + 1)
                        for b in range(nb(g)):
                            k = c * nb(g) + b
                            o = bank(ring_up(g, m) + k, ring_up(g, m0) + k)
                            w = 512 if b == 0 else NS
                            n = 0
                            for kd in range(KD):
                                for wt, x in ((up_hi, x_hi), (up_hi, x_lo), (up_lo, x_hi)):
                                    mm = pe.matmul(o[:, 0:w], wt[:, c % 2, kd * P:(kd + 1) * P], x[:, kd, 512 * b:512 * b + w],
                                                   start=n == 0, stop=n == 3 * KD - 1)
                                    n += 1
                            mm.then_inc(ring_full, 1)
                    if not first(m):
                        pe.wait_ge(h_lo_ok, hid0(g) + KQ * nb(g) * m)
                        down(g, m - 1, ring_up(g, m) + KQ * nb(g), ring_up(g, m0) + KQ * nb(g), (m0 - 1) % 2)

                for g in range(NG):
                    T = tiles(g)
                    for k in range(2):
                        down(g, k - 2, ring0(g) + 2 * T * k, ring0(g) + 2 * T * k, k)
                    for i in range(T):
                        t = tile0(g) + i
                        pe.wait_ge(xn_ok, t + 1)
                        for b in range(2):
                            wait(pe, x_lo_ok, KD * (t - 1) + 4 * (b + 1))
                            for q in range(4):
                                mm = pe.transpose(tp[b][:, q, :], acc[:, i, (4 * b + q) * P:(4 * b + q + 1) * P], ident[:])
                            mm.then_inc(tp_full, 1)
                    pe.wait_ge(x_lo_ok, KD * (tile0(g) + T))
                    steps(pe, g, step)
                    pe.wait_ge(h_lo_ok, hid0(g) + KQ * nb(g) * NSTEP)
                    e = ring_down(g, NSTEP - 1) - 2 * T
                    down(g, NSTEP - 1, e, e, (NSTEP - 1) % 2)


def hybrid_layer(nc, A):
    A = dict(A)
    A["u_d"] = nc.dram_tensor("u_d", (NTOK, G * GC), F32).ap()
    q_d = nc.dram_tensor("q_d", (NT, P, 4 * P), F32).ap()
    qi_d = nc.dram_tensor("qi_d", (NT, P, 2 * P), F32).ap()
    A["wi_d"] = nc.dram_tensor("wi_d", (NS, NIH), F32).ap()
    A["a_d"] = nc.dram_tensor("a_d", (NT, P, 4, P), F32).ap()
    A["so_d"] = nc.dram_tensor("so_d", (NT, P, 4, P), F32).ap()
    with ExitStack() as ctx:
        ident = ctx.enter_context(nc.sbuf_tensor("ident_sb", [P, P], F32))
        ident_ld, wi_st = ctx.enter_context(nc.semaphore("ident_ld")), ctx.enter_context(nc.semaphore("wi_st"))
        with nc.Block() as block:
            @block.sync
            def _(sp):
                sp.dma_start(ident[:], A["ident"]).then_inc(ident_ld, 16)
                sp.wait_ge(ident_ld, 16)
        with ExitStack() as keep:
            R = {name: keep.enter_context(nc.sbuf_tensor(name + "_sb", shape, F32)) for name, shape in (
                ("kT", [P, NTOK]), ("kiT", [P, NTOK]), ("V", [P, NT, P]), ("wi", [P, NT, NIH]),
                ("qk_s", [NS, NH + NKV, HD]), ("qi_s", [NS, NIH + 2, HD]))}
            project_inputs(nc, {**A, "q_d": q_d, "qi_d": qi_d}, R, ident)
            with nc.Block() as block:
                @block.sync
                def _(sp):
                    sp.dma_start(A["wi_d"], R["wi"][0:NS, NPT, :]).then_inc(wi_st, 16)
                    sp.wait_ge(wi_st, 16)
            A["q_d"] = q_d.rearrange("t p (a q) -> t p a q", a=4)
            A["qi_d"] = qi_d.rearrange("t p (a q) -> t p a q", a=2)
            R["mask_s"] = keep.enter_context(nc.sbuf_tensor("mask_s_sb", [NS, PAST + DECT], F32))
            attend(nc, A, R, ident)
            attend_samples(nc, A, R, ident)
        state_space(nc, A, R, ident)
        mix_and_feed_forward(nc, A, R, ident)


_OUTS = {"y_p": (SEQ, D), "y_s": (NS, D), "k_p": (SEQ, NKV * HD), "v_p": (SEQ, NKV * HD), "ki_p": (SEQ, HD),
         "hp_re": (P, GP), "hp_im": (P, GP), "k_s": (NS, NKV * HD), "v_s": (NS, NKV * HD), "ki_s": (NS, HD),
         "hs_re": (P, GP, DECB), "hs_im": (P, GP, DECB)}


def _layout(a):
    f = np.float32
    by_state = lambda z: z.reshape(GP, 2, SS, *z.shape[2:]).transpose(1, 2, 0, *range(3, z.ndim + 1)).reshape(P, GP, *z.shape[2:])
    x = np.concatenate([a["x_prompt"].reshape(-1, D), a["x_sample"].reshape(-1, D), np.zeros((NTOK - SEQ - NS, D), f)])
    w = a["w_in"][0]
    w_q = w[:, :OFF_K].reshape(D, NKV, QPK, HD).transpose(0, 2, 1, 3).reshape(D, OFF_K)
    pos = np.concatenate([np.arange(SEQ), np.tile(PAST + np.arange(DECT), P // DECT)]).astype(f)
    ang = (pos[:, None] * (10000.0 ** (-np.arange(HD // 2) / (HD // 2))).astype(f)).astype(np.float64)
    cos, sin = np.cos(ang), np.sin(ang)
    h0 = {}
    for n, k in (("h0_re", "state_ssm_re"), ("h0_im", "state_ssm_im")):
        h0[n] = np.zeros((P, GP, 16), f)
        h0[n][:, :, :DECB] = by_state(a[k][0].transpose(1, 2, 0))
    sel = np.zeros((4, NIH, DECT, 2, DECB, DECT), f)
    rep = np.zeros((DECB, DECT, DECB, NH, DECT), f)
    for b in range(DECB):
        for t in range(DECT):
            sel[b % 4, :, t, b // 4, b, t] = 1
            rep[b, t, b, :, t] = 1
    newmask = np.where(np.arange(DECT)[None] <= np.arange(DECT)[:, None], 0, NEG).astype(f)
    return {
        "ident": np.eye(P, dtype=f), "x_all": x, "xT_all": x.reshape(NT, P, KD, P).transpose(0, 3, 2, 1),
        "g_pre": a["norm_mix_pre"][0].reshape(KD, P).T, "w_in": np.concatenate([w_q, w[:, OFF_K:]], 1),
        "rope": np.concatenate([cos, cos, -sin, sin], 1).astype(f),
        "lam_re": by_state(a["lambda_re"][0]), "lam_im": by_state(a["lambda_im"][0]),
        "log_dt": by_state(np.repeat(a["log_dt"][0][:, None], SS, 1)),
        "b_re": by_state(a["b_re"][0]), "b_im": by_state(a["b_im"][0]),
        "c_re": by_state(a["c_re"][0].transpose(0, 2, 1)), "c_im": by_state(a["c_im"][0].transpose(0, 2, 1)),
        "d_skip": a["d_skip"][0].reshape(G, GC).T, "b_glu": a["b_glu"][0].reshape(4, P).T,
        "w_glu": a["w_glu"][0].reshape(4, P, G * GC).transpose(1, 0, 2), **h0,
        "page_table": a["page_table"].reshape(1, -1),
        "kidxT_pages": a["cache_kidx"][0].transpose(0, 2, 1),
        "kv_pages": np.stack([a["cache_k"][0].reshape(-1, PAGE, NKV * HD).transpose(0, 2, 1),
                              a["cache_v"][0].reshape(-1, PAGE, NKV * HD)], 2),
        "sel": sel.reshape(P, 2, NS), "rep": rep.reshape(NS, DECB, NS), "newmask": np.tile(newmask, (DECB, 1)),
        "w_out": a["w_out"][0].reshape(KD, P, D),
        "w_up": a["w_up"][0].reshape(KD, P, DFF // P, P).transpose(2, 1, 0, 3).reshape(DFF // P, P, D),
        "w_down": a["w_down"][0].reshape(DFF // P, P, D),
        "g_post": np.tile(a["norm_mix_post"][0], (P, 1)), "g_ffn": np.tile(a["norm_ffn_post"][0], (P, 1)),
        "g_ffn_pre": a["norm_ffn_pre"][0].reshape(KD, P).T,
    }


def kernel(**inputs):
    import concourse.bacc as _bacc
    from concourse.bass_utils import run_bass_kernel_spmd as _run

    nc = _bacc.Bacc("TRN2", target_bir_lowering=False, num_devices=1)
    arrays = {n: np.ascontiguousarray(a) for n, a in _layout({n: np.asarray(a) for n, a in inputs.items()}).items()}
    args = {n: nc.dram_tensor(n, a.shape, mybir.dt.from_np(a.dtype), kind="ExternalInput").ap() for n, a in arrays.items()}
    args.update({n: nc.dram_tensor(n, shape, F32, kind="ExternalOutput").ap() for n, shape in _OUTS.items()})
    hybrid_layer(nc, args)
    r = _run(nc, [arrays], core_ids=[0]).results[0]
    by_group = lambda z: z.reshape(2, SS, GP, *z.shape[2:]).transpose(2, 0, 1, *range(3, z.ndim + 1)).reshape(G, SS, *z.shape[2:])
    return (r["y_p"].reshape(1, SEQ, D), r["y_s"].reshape(DECB, DECT, D),
            r["k_p"].reshape(1, 1, SEQ, NKV, HD), r["v_p"].reshape(1, 1, SEQ, NKV, HD), r["ki_p"].reshape(1, 1, SEQ, HD),
            by_group(r["hp_re"])[None, None], by_group(r["hp_im"])[None, None],
            r["k_s"].reshape(1, DECB, DECT, NKV, HD), r["v_s"].reshape(1, DECB, DECT, NKV, HD),
            r["ki_s"].reshape(1, DECB, DECT, HD),
            by_group(r["hs_re"]).transpose(2, 0, 1)[None], by_group(r["hs_im"]).transpose(2, 0, 1)[None])
```
